# Optimizing a Trainium2 kernel written in Bass

```python
import jax, jax.numpy as jnp
from jax import lax
import numpy as np
import math
import jax
import jax.numpy as jnp

D_MODEL = 1024
BATCH = 1
SEQ = 256
DEPTH = 2

GRID_W = 64
CTX_LEN = 256
HEAD_DIM = 64
MIX_WIDTH = D_MODEL
A_HEADS = 6
A_KV = 2
A_WINDOW = 128
A_BLOCK = 128
B_HEADS = 4
B_KV = 2
B_BLOCK = 128
C_HEADS = 6
NA_KH = 8
NA_KW = 16
D_FF = 2816
ROPE_THETA = 10000.0
EPS = 1e-6
N_MOD = 9
NEG = -1e30
KV_WIDTHS = (A_KV, A_KV, B_KV, B_KV, C_HEADS, C_HEADS)
W_IN_COLS = MIX_WIDTH + sum(KV_WIDTHS) * HEAD_DIM


def _rms_norm(x, g):
    xf = x.astype(jnp.float32)
    y = xf * lax.rsqrt(jnp.mean(xf * xf, axis=-1, keepdims=True) + EPS)
    return (y * g.astype(jnp.float32)).astype(x.dtype)

def _modulate(u, shift, scale):
    return u * (1.0 + scale) + shift

def _swiglu(u, w_gate, w_up, w_down):
    return (jax.nn.silu(u @ w_gate) * (u @ w_up)) @ w_down

def _axial_rope(S):
    t = jnp.arange(S)
    row = (t // GRID_W).astype(jnp.float32)
    col = (t % GRID_W).astype(jnp.float32)
    n_freq = HEAD_DIM // 4
    inv = ROPE_THETA ** (-jnp.arange(n_freq, dtype=jnp.float32) / n_freq)
    ang = jnp.concatenate([row[:, None] * inv, col[:, None] * inv], axis=-1)
    return jnp.cos(ang), jnp.sin(ang)

def _rope(x, cos, sin):
    half = HEAD_DIM // 2
    x1, x2 = x[..., :half], x[..., half:]
    cs, sn = cos[None, :, None, :], sin[None, :, None, :]
    return jnp.concatenate([x1 * cs - x2 * sn, x2 * cs + x1 * sn], axis=-1).astype(x.dtype)

def _multi_softmax(logits):
    sizes = [int(l.shape[-1]) for l in logits]
    p = jax.nn.softmax(jnp.concatenate(logits, axis=-1), axis=-1)
    return jnp.split(p, [int(s) for s in np.cumsum(sizes)[:-1]], axis=-1)

def _heads(t, n):
    return t.reshape(*t.shape[:-1], n, HEAD_DIM)

def _split_q(p):
    a = A_HEADS * HEAD_DIM
    b = B_HEADS * HEAD_DIM
    return (_heads(p[..., :a], A_HEADS), _heads(p[..., a:a + b], B_HEADS),
            _heads(p[..., a + b:MIX_WIDTH], C_HEADS))

def _split_kv(p):
    offs = [0]
    for w in KV_WIDTHS:
        offs.append(offs[-1] + w * HEAD_DIM)
    return [_heads(p[..., offs[i]:offs[i + 1]], KV_WIDTHS[i]) for i in range(len(KV_WIDTHS))]

def _ctx_attn(qc, kc, vc, sink=None):
    Bn, L, H, d = qc.shape
    KV = kc.shape[2]
    G = H // KV
    qg = qc.reshape(Bn, L, KV, G, d)
    s = jnp.einsum('bqkgd,blkd->bkgql', qg, kc).astype(jnp.float32) * (d ** -0.5)
    if sink is None:
        p = jax.nn.softmax(s, axis=-1)
    else:
        sink_col = jnp.broadcast_to(sink.astype(jnp.float32).reshape(1, KV, G, 1, 1), (Bn, KV, G, L, 1))
        p, _ = _multi_softmax([s, sink_col])
    out = jnp.einsum('bkgql,blkd->bqkgd', p.astype(vc.dtype), vc)
    return out.reshape(Bn, L, H * d)

def _window_attn(q, k, v, kc, vc, sink):
    Bn, S, H, d = q.shape
    KV = k.shape[2]
    G = H // KV
    nb = S // A_BLOCK
    band = 3 * A_BLOCK
    scale = d ** -0.5
    pad = ((0, 0), (A_BLOCK, A_BLOCK), (0, 0), (0, 0))
    kp, vp = jnp.pad(k, pad), jnp.pad(v, pad)
    qb = jnp.moveaxis(q.reshape(Bn, nb, A_BLOCK, KV, G, d), 1, 0)
    rel = jnp.arange(band)[None, :] - A_BLOCK - jnp.arange(A_BLOCK)[:, None]
    sink_col = jnp.broadcast_to(sink.astype(jnp.float32).reshape(1, KV, G, 1, 1), (Bn, KV, G, A_BLOCK, 1))

    def block(args):
        n, q_n = args
        start = n * A_BLOCK
        k_n = lax.dynamic_slice_in_dim(kp, start, band, axis=1)
        v_n = lax.dynamic_slice_in_dim(vp, start, band, axis=1)
        kpos = start - A_BLOCK + jnp.arange(band)
        mask = (jnp.abs(rel) <= A_WINDOW) & ((kpos >= 0) & (kpos < S))[None, :]
        s_w = jnp.einsum('bqkgd,bskd->bkgqs', q_n, k_n).astype(jnp.float32) * scale
        s_w = jnp.where(mask, s_w, NEG)
        s_c = jnp.einsum('bqkgd,blkd->bkgql', q_n, kc).astype(jnp.float32) * scale
        p_w, p_c, _ = _multi_softmax([s_w, s_c, sink_col])
        return (jnp.einsum('bkgqs,bskd->bqkgd', p_w.astype(v.dtype), v_n)
                + jnp.einsum('bkgql,blkd->bqkgd', p_c.astype(vc.dtype), vc))

    out = lax.map(block, (jnp.arange(nb), qb))
    return jnp.moveaxis(out, 0, 1).reshape(Bn, S, H * d)

def _global_attn(q, k, v, kc, vc):
    Bn, S, H, d = q.shape
    KV = k.shape[2]
    G = H // KV
    nb = S // B_BLOCK
    scale = d ** -0.5
    qb = jnp.moveaxis(q.reshape(Bn, nb, B_BLOCK, KV, G, d), 1, 0)

    def block(q_n):
        s_l = jnp.einsum('bqkgd,bskd->bkgqs', q_n, k).astype(jnp.float32) * scale
        s_c = jnp.einsum('bqkgd,blkd->bkgql', q_n, kc).astype(jnp.float32) * scale
        p_l, p_c = _multi_softmax([s_l, s_c])
        return (jnp.einsum('bkgqs,bskd->bqkgd', p_l.astype(v.dtype), v)
                + jnp.einsum('bkgql,blkd->bqkgd', p_c.astype(vc.dtype), vc))

    out = lax.map(block, qb)
    return jnp.moveaxis(out, 0, 1).reshape(Bn, S, H * d)

def _neighbourhood_attn(q, k, v, kc, vc, rpb):
    Bn, S, H, d = q.shape
    rows = S // GRID_W
    kh = min(NA_KH, rows)
    kw = NA_KW
    n_keys = kh * kw
    scale = d ** -0.5
    qg = jnp.moveaxis(q.reshape(Bn, rows, GRID_W, H, d), 1, 0)
    kg = k.reshape(Bn, rows, GRID_W, H, d)
    vg = v.reshape(Bn, rows, GRID_W, H, d)
    cols = np.arange(GRID_W)
    col_idx = np.clip(cols - kw // 2, 0, GRID_W - kw)[:, None] + np.arange(kw)[None, :]
    dc = col_idx - cols[:, None] + NA_KW - 1
    rpb_col = rpb[:, :, dc]

    def gather(t, rs):
        t_rows = lax.dynamic_slice_in_dim(t, rs, kh, axis=1)
        t_nb = t_rows[:, :, col_idx]
        return jnp.transpose(t_nb, (0, 2, 1, 3, 4, 5)).reshape(Bn, GRID_W, n_keys, H, d)

    def block(args):
        r, q_r = args
        rs = jnp.clip(r - kh // 2, 0, rows - kh)
        dr = rs + jnp.arange(kh) - r + NA_KH - 1
        bias = jnp.transpose(jnp.take(rpb_col, dr, axis=1), (0, 2, 1, 3)).reshape(H, GRID_W, n_keys)
        k_nb, v_nb = gather(kg, rs), gather(vg, rs)
        s_n = jnp.einsum('bwhd,bwnhd->bhwn', q_r, k_nb).astype(jnp.float32) * scale + bias.astype(jnp.float32)
        s_c = jnp.einsum('bwhd,blhd->bhwl', q_r, kc).astype(jnp.float32) * scale
        p_n, p_c = _multi_softmax([s_n, s_c])
        return (jnp.einsum('bhwn,bwnhd->bwhd', p_n.astype(v.dtype), v_nb)
                + jnp.einsum('bhwl,blhd->bwhd', p_c.astype(vc.dtype), vc))

    out = lax.map(block, (jnp.arange(rows), qg))
    return jnp.moveaxis(out, 0, 1).reshape(Bn, S, H * d)

def first_inputs(seed: int = 0) -> dict:
    key = jax.random.key(seed)
    ks = jax.random.split(key, 24)
    f32 = jnp.float32
    D, F = D_MODEL, D_FF

    def nrm(k, shape, s):
        return jax.random.normal(k, shape, f32) * s

    def gain(k, shape):
        return 1.0 + 0.02 * jax.random.normal(k, shape, f32)

    return {
        "x": nrm(ks[0], (BATCH, SEQ, D), 1.0),
        "c": nrm(ks[1], (BATCH, D), 1.0),
        "ctx": nrm(ks[2], (BATCH, CTX_LEN, D), 1.0),
        "c_ctx": nrm(ks[3], (D,), 1.0),
        "w_ada": nrm(ks[4], (DEPTH, D, N_MOD * D), 0.5 * D ** -0.5),
        "b_ada": nrm(ks[5], (DEPTH, N_MOD * D), 0.02),
        "norm_ffn1": gain(ks[6], (DEPTH, D)),
        "w_ffn1_gate": nrm(ks[7], (DEPTH, D, F), D ** -0.5),
        "w_ffn1_up": nrm(ks[8], (DEPTH, D, F), D ** -0.5),
        "w_ffn1_down": nrm(ks[9], (DEPTH, F, D), F ** -0.5),
        "norm_mix": gain(ks[10], (DEPTH, D)),
        "w_in": nrm(ks[11], (DEPTH, D, W_IN_COLS), D ** -0.5),
        "q_norm_glob": gain(ks[12], (DEPTH, HEAD_DIM)),
        "k_norm_glob": gain(ks[13], (DEPTH, HEAD_DIM)),
        "sink_win": nrm(ks[14], (DEPTH, A_HEADS), 0.5),
        "rpb_nbr": nrm(ks[15], (DEPTH, C_HEADS, 2 * NA_KH - 1, 2 * NA_KW - 1), 0.1),
        "w_out": nrm(ks[16], (DEPTH, MIX_WIDTH, D), MIX_WIDTH ** -0.5),
        "norm_ffn2": gain(ks[17], (DEPTH, D)),
        "w_ffn2_gate": nrm(ks[18], (DEPTH, D, F), D ** -0.5),
        "w_ffn2_up": nrm(ks[19], (DEPTH, D, F), D ** -0.5),
        "w_ffn2_down": nrm(ks[20], (DEPTH, F, D), F ** -0.5),
        "norm_final": gain(ks[21], (D,)),
    }

def first_block(x, c, ctx, c_ctx, w_ada, b_ada, norm_ffn1, w_ffn1_gate, w_ffn1_up, w_ffn1_down,
              norm_mix, w_in, q_norm_glob, k_norm_glob, sink_win, rpb_nbr, w_out,
              norm_ffn2, w_ffn2_gate, w_ffn2_up, w_ffn2_down, norm_final):
    S = x.shape[1]
    cos, sin = _axial_rope(S)
    h, hc = x, ctx
    for l in range(DEPTH):
        last = l == DEPTH - 1
        mod_x = (jax.nn.silu(c) @ w_ada[l] + b_ada[l])[:, None, :]
        mod_c = jax.nn.silu(c_ctx) @ w_ada[l] + b_ada[l]
        sh1, sc1, g1, shm, scm, gm, sh2, sc2, g2 = jnp.split(mod_x, N_MOD, axis=-1)
        csh1, csc1, cg1, cshm, cscm, cgm, csh2, csc2, cg2 = jnp.split(mod_c, N_MOD, axis=-1)

        h = h + 0.5 * g1 * _swiglu(_modulate(_rms_norm(h, norm_ffn1[l]), sh1, sc1),
                                   w_ffn1_gate[l], w_ffn1_up[l], w_ffn1_down[l])
        hc = hc + 0.5 * cg1 * _swiglu(_modulate(_rms_norm(hc, norm_ffn1[l]), csh1, csc1),
                                      w_ffn1_gate[l], w_ffn1_up[l], w_ffn1_down[l])

        u = _modulate(_rms_norm(h, norm_mix[l]), shm, scm)
        uc = _modulate(_rms_norm(hc, norm_mix[l]), cshm, cscm)
        p = u @ w_in[l]
        q_w, q_g, q_n = _split_q(p[..., :MIX_WIDTH])
        k_w, v_w, k_g, v_g, k_n, v_n = _split_kv(p[..., MIX_WIDTH:])
        if last:
            kv_c = uc @ w_in[l][:, MIX_WIDTH:]
        else:
            pc = uc @ w_in[l]
            cq_w, cq_g, cq_n = _split_q(pc[..., :MIX_WIDTH])
            kv_c = pc[..., MIX_WIDTH:]
        ck_w, cv_w, ck_g, cv_g, ck_n, cv_n = _split_kv(kv_c)

        q_g = _rms_norm(q_g, q_norm_glob[l])
        k_g = _rms_norm(k_g, k_norm_glob[l])
        ck_g = _rms_norm(ck_g, k_norm_glob[l])
        q_w, k_w = _rope(q_w, cos, sin), _rope(k_w, cos, sin)
        q_g, k_g = _rope(q_g, cos, sin), _rope(k_g, cos, sin)

        y_w = _window_attn(q_w, k_w, v_w, ck_w, cv_w, sink_win[l])
        y_g = _global_attn(q_g, k_g, v_g, ck_g, cv_g)
        y_n = _neighbourhood_attn(q_n, k_n, v_n, ck_n, cv_n, rpb_nbr[l])
        h = h + gm * (jnp.concatenate([y_w, y_g, y_n], axis=-1) @ w_out[l])

        if not last:
            cq_g = _rms_norm(cq_g, q_norm_glob[l])
            yc = jnp.concatenate([_ctx_attn(cq_w, ck_w, cv_w, sink_win[l]),
                                  _ctx_attn(cq_g, ck_g, cv_g),
                                  _ctx_attn(cq_n, ck_n, cv_n)], axis=-1)
            hc = hc + cgm * (yc @ w_out[l])

        h = h + 0.5 * g2 * _swiglu(_modulate(_rms_norm(h, norm_ffn2[l]), sh2, sc2),
                                   w_ffn2_gate[l], w_ffn2_up[l], w_ffn2_down[l])
        if not last:
            hc = hc + 0.5 * cg2 * _swiglu(_modulate(_rms_norm(hc, norm_ffn2[l]), csh2, csc2),
                                          w_ffn2_gate[l], w_ffn2_up[l], w_ffn2_down[l])
    return _rms_norm(h, norm_final)


DEPTH_2 = 1

RWKV_HEADS = 8
RWKV_HEAD_DIM = 64
RWKV_DIM = RWKV_HEADS * RWKV_HEAD_DIM
RWKV_W_LORA = 64
RWKV_A_LORA = 64
RWKV_G_LORA = 128
RWKV_GN_EPS = 64e-5
MLA_HEADS = 8
MLA_Q_LORA = 256
MLA_KV_LORA = 128
MLA_NOPE_DIM = 64
MLA_ROPE_DIM = 32
MLA_V_DIM = 64
MLA_DIM = MLA_HEADS * MLA_V_DIM
ROPE_BASE = 10000.0
DIFF_HEADS = 4
DIFF_QK_DIM = 64
DIFF_V_DIM = 2 * DIFF_QK_DIM
DIFF_DIM = DIFF_HEADS * DIFF_V_DIM
REL_BUCKETS = 32
REL_MAX_DISTANCE = 128
CONV_WIDTH = 3
N_BRANCHES = 3
Q_BLOCK = 128
NORM_EPS = 1e-6

RWKV_COLS = 3 * RWKV_DIM + RWKV_W_LORA + RWKV_A_LORA + RWKV_G_LORA
MLA_COLS = MLA_Q_LORA + MLA_KV_LORA + MLA_ROPE_DIM
DIFF_COLS = 2 * (DIFF_HEADS * 2 * DIFF_QK_DIM) + DIFF_DIM
GATE_COLS = N_BRANCHES * D_MODEL
IN_COLS = RWKV_COLS + MLA_COLS + DIFF_COLS + GATE_COLS
IN_SPLITS = (RWKV_COLS, RWKV_COLS + MLA_COLS, RWKV_COLS + MLA_COLS + DIFF_COLS)
RWKV_SPLITS = (RWKV_DIM, 2 * RWKV_DIM, 3 * RWKV_DIM, 3 * RWKV_DIM + RWKV_W_LORA,
               3 * RWKV_DIM + RWKV_W_LORA + RWKV_A_LORA)


def _rmsnorm(x, g, eps=NORM_EPS):
    xf = x.astype(jnp.float32)
    y = xf * lax.rsqrt(jnp.mean(xf * xf, axis=-1, keepdims=True) + eps)
    return (y * g.astype(jnp.float32)).astype(x.dtype)

def _token_shift(p):
    return jnp.pad(p, ((0, 0), (1, 0), (0, 0)))[:, :-1]

def _split_heads(t, n_heads):
    return t.reshape(t.shape[0], t.shape[1], n_heads, t.shape[-1] // n_heads)

def _rope_tables(positions, dtype):
    inv_freq = ROPE_BASE ** (-jnp.arange(0, MLA_ROPE_DIM, 2, dtype=jnp.float32) / MLA_ROPE_DIM)
    ang = positions.astype(jnp.float32)[..., None] * inv_freq
    return jnp.cos(ang).astype(dtype), jnp.sin(ang).astype(dtype)

def _apply_rope(x, cos, sin):
    x1, x2 = jnp.split(x, 2, axis=-1)
    return jnp.concatenate([x1 * cos - x2 * sin, x1 * sin + x2 * cos], axis=-1)

def _t5_bucket(dist):
    n = jnp.maximum(dist, 0)
    max_exact = REL_BUCKETS // 2
    nf = jnp.maximum(n, 1).astype(jnp.float32)
    large = max_exact + (jnp.log(nf / max_exact) / math.log(REL_MAX_DISTANCE / max_exact)
                         * (REL_BUCKETS - max_exact)).astype(jnp.int32)
    large = jnp.minimum(large, REL_BUCKETS - 1)
    return jnp.where(n < max_exact, n, large)

def _masked_softmax(logits, mask):
    logits = jnp.where(mask, logits.astype(jnp.float32), jnp.finfo(jnp.float32).min)
    return jax.nn.softmax(logits, axis=-1)

def _causal_blocks(block_fn, seq_len):
    outs = []
    for i in range(seq_len // Q_BLOCK):
        q0, q1 = i * Q_BLOCK, (i + 1) * Q_BLOCK
        mask = jnp.arange(q0, q1)[:, None] >= jnp.arange(q1)[None, :]
        outs.append(block_fn(q0, q1, mask))
    return jnp.concatenate(outs, axis=2)

def _rwkv7_mix(p, mu, w0, w2, a0, a2, g2, k_k, k_a, r_k, ln_w, ln_b):
    B, S, _ = p.shape
    f32 = jnp.float32
    p = p + (_token_shift(p) - p) * mu
    r, k, v, pw, pa, pg = jnp.split(p, RWKV_SPLITS, axis=-1)
    w_log = -jax.nn.softplus(-(w0 + jnp.tanh(pw) @ w2)) - 0.5
    decay = jnp.exp(-jnp.exp(w_log.astype(f32)))
    a = jax.nn.sigmoid(a0 + pa @ a2)
    g = jax.nn.sigmoid(pg) @ g2
    kk = _split_heads(k * k_k, RWKV_HEADS).astype(f32)
    kk = kk / jnp.maximum(jnp.linalg.norm(kk, axis=-1, keepdims=True), 1e-12)
    k = k * (1 + (a - 1) * k_a)
    r_h, k_h, v_h = _split_heads(r, RWKV_HEADS), _split_heads(k, RWKV_HEADS), _split_heads(v, RWKV_HEADS)
    b_h = kk * _split_heads(a, RWKV_HEADS).astype(f32)
    xs = tuple(jnp.moveaxis(t.astype(f32), 1, 0)
               for t in (r_h, _split_heads(decay, RWKV_HEADS), k_h, v_h, kk, b_h))

    def step(state, inp):
        r_t, w_t, k_t, v_t, kk_t, b_t = inp
        sa = jnp.einsum('bhij,bhj->bhi', state, -kk_t)
        state = (state * w_t[:, :, None, :] + sa[..., None] * b_t[:, :, None, :]
                 + v_t[..., None] * k_t[:, :, None, :])
        return state, jnp.einsum('bhij,bhj->bhi', state, r_t)

    state0 = jnp.zeros((B, RWKV_HEADS, RWKV_HEAD_DIM, RWKV_HEAD_DIM), f32)
    _, y = lax.scan(step, state0, xs)
    y = jnp.moveaxis(y, 0, 1)
    mean = jnp.mean(y, axis=-1, keepdims=True)
    var = jnp.mean(jnp.square(y - mean), axis=-1, keepdims=True)
    y = ((y - mean) * lax.rsqrt(var + RWKV_GN_EPS)).reshape(B, S, RWKV_DIM) * ln_w + ln_b
    bonus = (jnp.sum(r_h * k_h * r_k, axis=-1, keepdims=True) * v_h).reshape(B, S, RWKV_DIM)
    y = (y + bonus.astype(f32)) * g.astype(f32)
    return y.astype(p.dtype)

def _mla_mix(p, cos, sin, q_norm, w_uq, kv_norm, w_ukv):
    B, S, _ = p.shape
    c_q, c_kv, k_rope = jnp.split(p, (MLA_Q_LORA, MLA_Q_LORA + MLA_KV_LORA), axis=-1)
    q = (_rmsnorm(c_q, q_norm) @ w_uq).reshape(B, S, MLA_HEADS, MLA_NOPE_DIM + MLA_ROPE_DIM)
    q = q.transpose(0, 2, 1, 3)
    q_nope = q[..., :MLA_NOPE_DIM]
    q_rope = _apply_rope(q[..., MLA_NOPE_DIM:], cos[:, None], sin[:, None])
    kv = (_rmsnorm(c_kv, kv_norm) @ w_ukv).reshape(B, S, MLA_HEADS, MLA_NOPE_DIM + MLA_V_DIM)
    kv = kv.transpose(0, 2, 1, 3)
    k_nope, v = kv[..., :MLA_NOPE_DIM], kv[..., MLA_NOPE_DIM:]
    k_rope = _apply_rope(k_rope, cos, sin)
    scale = (MLA_NOPE_DIM + MLA_ROPE_DIM) ** -0.5

    def block(q0, q1, mask):
        logits = (jnp.einsum('bhqd,bhkd->bhqk', q_nope[:, :, q0:q1], k_nope[:, :, :q1])
                  + jnp.einsum('bhqd,bkd->bhqk', q_rope[:, :, q0:q1], k_rope[:, :q1]))
        probs = _masked_softmax(logits * scale, mask)
        return jnp.einsum('bhqk,bhkd->bhqd', probs.astype(v.dtype), v[:, :, :q1])

    o = _causal_blocks(block, S)
    return o.transpose(0, 2, 1, 3).reshape(B, S, MLA_DIM)

def _diff_mix(p, positions, rel_bias, lam, subln, layer_idx):
    B, S, _ = p.shape
    qk_w = DIFF_HEADS * 2 * DIFF_QK_DIM
    q, k, v = jnp.split(p, (qk_w, 2 * qk_w), axis=-1)
    q = q.reshape(B, S, DIFF_HEADS, 2, DIFF_QK_DIM).transpose(0, 2, 3, 1, 4)
    k = k.reshape(B, S, DIFF_HEADS, 2, DIFF_QK_DIM).transpose(0, 2, 3, 1, 4)
    v = v.reshape(B, S, DIFF_HEADS, DIFF_V_DIM).transpose(0, 2, 1, 3)
    lambda_init = 0.8 - 0.6 * math.exp(-0.3 * layer_idx)
    lam = lam.astype(jnp.float32)
    lam_full = jnp.exp(jnp.sum(lam[0] * lam[1])) - jnp.exp(jnp.sum(lam[2] * lam[3])) + lambda_init
    scale = DIFF_QK_DIM ** -0.5

    def block(q0, q1, mask):
        dist = positions[:, q0:q1, None] - positions[:, None, :q1]
        bias = rel_bias[_t5_bucket(dist)].transpose(0, 3, 1, 2)[:, :, None]
        logits = jnp.einsum('bhmqd,bhmkd->bhmqk', q[:, :, :, q0:q1], k[:, :, :, :q1]) * scale + bias
        probs = _masked_softmax(logits, mask)
        attn = probs[:, :, 0] - lam_full * probs[:, :, 1]
        return jnp.einsum('bhqk,bhkd->bhqd', attn.astype(v.dtype), v[:, :, :q1])

    o = _causal_blocks(block, S)
    o = _rmsnorm(o, subln, eps=1e-5) * (1 - lambda_init)
    return o.transpose(0, 2, 1, 3).reshape(B, S, DIFF_DIM)

def _conv_ffn(h, w_up, conv_w, conv_b, w_down):
    S = h.shape[1]
    u = h @ w_up
    up = jnp.pad(u, ((0, 0), (CONV_WIDTH - 1, 0), (0, 0)))
    u = sum(conv_w[j] * up[:, j:j + S] for j in range(CONV_WIDTH)) + conv_b
    gate, val = jnp.split(u, 2, axis=-1)
    return (jax.nn.silu(gate) * val) @ w_down

def second_inputs(seed: int = 0) -> dict:
    key = jax.random.key(seed)
    ks = iter(jax.random.split(key, 40))
    f32 = jnp.float32
    L = DEPTH_2

    def nrm(shape, scale):
        return jax.random.normal(next(ks), shape, f32) * scale

    def gain(shape):
        return 1.0 + nrm(shape, 0.05)

    offset = jax.random.randint(next(ks), (BATCH, 1), 0, 1024, dtype=jnp.int32)
    positions = offset + jnp.arange(SEQ, dtype=jnp.int32)[None, :]
    return {
        'x': nrm((BATCH, SEQ, D_MODEL), 1.0),
        'positions': positions,
        'rel_bias': nrm((REL_BUCKETS, DIFF_HEADS), 0.5),
        'norm_mix': gain((L, D_MODEL)),
        'w_in': nrm((L, D_MODEL, IN_COLS), D_MODEL ** -0.5),
        'b_gate': nrm((L, GATE_COLS), 0.1),
        'rwkv_mu': jax.random.uniform(next(ks), (L, RWKV_COLS), f32),
        'rwkv_w0': jax.random.uniform(next(ks), (L, RWKV_DIM), f32, minval=-6.0, maxval=-1.0),
        'rwkv_w2': nrm((L, RWKV_W_LORA, RWKV_DIM), 0.1 * RWKV_W_LORA ** -0.5),
        'rwkv_a0': nrm((L, RWKV_DIM), 0.1),
        'rwkv_a2': nrm((L, RWKV_A_LORA, RWKV_DIM), RWKV_A_LORA ** -0.5),
        'rwkv_g2': nrm((L, RWKV_G_LORA, RWKV_DIM), RWKV_G_LORA ** -0.5),
        'rwkv_k_k': 0.85 + nrm((L, RWKV_DIM), 0.05),
        'rwkv_k_a': gain((L, RWKV_DIM)),
        'rwkv_r_k': nrm((L, RWKV_HEADS, RWKV_HEAD_DIM), 0.1),
        'rwkv_ln_w': gain((L, RWKV_DIM)),
        'rwkv_ln_b': nrm((L, RWKV_DIM), 0.02),
        'mla_q_norm': gain((L, MLA_Q_LORA)),
        'mla_w_uq': nrm((L, MLA_Q_LORA, MLA_HEADS * (MLA_NOPE_DIM + MLA_ROPE_DIM)), MLA_Q_LORA ** -0.5),
        'mla_kv_norm': gain((L, MLA_KV_LORA)),
        'mla_w_ukv': nrm((L, MLA_KV_LORA, MLA_HEADS * (MLA_NOPE_DIM + MLA_V_DIM)), MLA_KV_LORA ** -0.5),
        'diff_lambda': nrm((L, 4, DIFF_QK_DIM), 0.1),
        'diff_subln': gain((L, DIFF_V_DIM)),
        'w_branch_rwkv': nrm((L, RWKV_DIM, D_MODEL), RWKV_DIM ** -0.5),
        'w_branch_mla': nrm((L, MLA_DIM, D_MODEL), MLA_DIM ** -0.5),
        'w_branch_diff': nrm((L, DIFF_DIM, D_MODEL), DIFF_DIM ** -0.5),
        'w_o': nrm((L, D_MODEL, D_MODEL), D_MODEL ** -0.5),
        'norm_ffn': gain((L, D_MODEL)),
        'ffn_w_up': nrm((L, D_MODEL, 2 * D_FF), D_MODEL ** -0.5),
        'ffn_conv_w': nrm((L, CONV_WIDTH, 2 * D_FF), CONV_WIDTH ** -0.5),
        'ffn_conv_b': nrm((L, 2 * D_FF), 0.02),
        'ffn_w_down': nrm((L, D_FF, D_MODEL), D_FF ** -0.5),
        'norm_final': gain((D_MODEL,)),
    }

def second_block(x, positions, rel_bias, norm_mix, w_in, b_gate, rwkv_mu, rwkv_w0, rwkv_w2, rwkv_a0,
              rwkv_a2, rwkv_g2, rwkv_k_k, rwkv_k_a, rwkv_r_k, rwkv_ln_w, rwkv_ln_b, mla_q_norm,
              mla_w_uq, mla_kv_norm, mla_w_ukv, diff_lambda, diff_subln, w_branch_rwkv, w_branch_mla,
              w_branch_diff, w_o, norm_ffn, ffn_w_up, ffn_conv_w, ffn_conv_b, ffn_w_down, norm_final):
    B, S, _ = x.shape
    cos, sin = _rope_tables(positions, x.dtype)
    for l in range(DEPTH_2):
        h = _rmsnorm(x, norm_mix[l])
        p = h @ w_in[l]
        p_rwkv, p_mla, p_diff, p_gate = jnp.split(p, IN_SPLITS, axis=-1)
        o_rwkv = _rwkv7_mix(p_rwkv, rwkv_mu[l], rwkv_w0[l], rwkv_w2[l], rwkv_a0[l], rwkv_a2[l],
                            rwkv_g2[l], rwkv_k_k[l], rwkv_k_a[l], rwkv_r_k[l], rwkv_ln_w[l], rwkv_ln_b[l])
        o_mla = _mla_mix(p_mla, cos, sin, mla_q_norm[l], mla_w_uq[l], mla_kv_norm[l], mla_w_ukv[l])
        o_diff = _diff_mix(p_diff, positions, rel_bias, diff_lambda[l], diff_subln[l], l)
        gates = jax.nn.sigmoid(p_gate + b_gate[l]).reshape(B, S, N_BRANCHES, D_MODEL)
        merged = (gates[:, :, 0] * (o_rwkv @ w_branch_rwkv[l])
                  + gates[:, :, 1] * (o_mla @ w_branch_mla[l])
                  + gates[:, :, 2] * (o_diff @ w_branch_diff[l]))
        x = x + merged @ w_o[l]
        x = x + _conv_ffn(_rmsnorm(x, norm_ffn[l]), ffn_w_up[l], ffn_conv_w[l], ffn_conv_b[l], ffn_w_down[l])
    return _rmsnorm(x, norm_final)


def setup_inputs(seed=0):
    out = dict(first_inputs(seed))
    for name, value in second_inputs(seed + 1).items():
        if name != "x":
            out[name + "_2"] = value
    return out


def reference(
    x, c, ctx, c_ctx, w_ada, b_ada, norm_ffn1, w_ffn1_gate, w_ffn1_up, w_ffn1_down, norm_mix,
    w_in, q_norm_glob, k_norm_glob, sink_win, rpb_nbr, w_out, norm_ffn2, w_ffn2_gate, w_ffn2_up,
    w_ffn2_down, norm_final, positions_2, rel_bias_2, norm_mix_2, w_in_2, b_gate_2, rwkv_mu_2,
    rwkv_w0_2, rwkv_w2_2, rwkv_a0_2, rwkv_a2_2, rwkv_g2_2, rwkv_k_k_2, rwkv_k_a_2, rwkv_r_k_2,
    rwkv_ln_w_2, rwkv_ln_b_2, mla_q_norm_2, mla_w_uq_2, mla_kv_norm_2, mla_w_ukv_2,
    diff_lambda_2, diff_subln_2, w_branch_rwkv_2, w_branch_mla_2, w_branch_diff_2, w_o_2,
    norm_ffn_2, ffn_w_up_2, ffn_conv_w_2, ffn_conv_b_2, ffn_w_down_2, norm_final_2,
):
    x = first_block(
        x, c, ctx, c_ctx, w_ada, b_ada, norm_ffn1, w_ffn1_gate, w_ffn1_up, w_ffn1_down,
        norm_mix, w_in, q_norm_glob, k_norm_glob, sink_win, rpb_nbr, w_out, norm_ffn2,
        w_ffn2_gate, w_ffn2_up, w_ffn2_down, norm_final,
    )
    return second_block(
        x, positions_2, rel_bias_2, norm_mix_2, w_in_2, b_gate_2, rwkv_mu_2, rwkv_w0_2,
        rwkv_w2_2, rwkv_a0_2, rwkv_a2_2, rwkv_g2_2, rwkv_k_k_2, rwkv_k_a_2, rwkv_r_k_2,
        rwkv_ln_w_2, rwkv_ln_b_2, mla_q_norm_2, mla_w_uq_2, mla_kv_norm_2, mla_w_ukv_2,
        diff_lambda_2, diff_subln_2, w_branch_rwkv_2, w_branch_mla_2, w_branch_diff_2, w_o_2,
        norm_ffn_2, ffn_w_up_2, ffn_conv_w_2, ffn_conv_b_2, ffn_w_down_2, norm_final_2,
    )


_drawn_inputs = setup_inputs


def setup_inputs(seed=0):
    import zlib

    import numpy as np

    out = dict(_drawn_inputs(seed))
    spreads = {}
    factors = {'norm_ffn1': 8.0,
     'norm_mix': 8.0,
     'q_norm_glob': 8.0,
     'k_norm_glob': 8.0,
     'sink_win': 8.0,
     'rpb_nbr': 8.0,
     'norm_ffn2': 8.0,
     'b_gate_2': 2.699,
     'rwkv_w2_2': 38.654,
     'rwkv_a0_2': 5.447,
     'rwkv_k_k_2': 22.506,
     'rwkv_k_a_2': 3.374,
     'rwkv_ln_w_2': 16.006,
     'rwkv_ln_b_2': 36.051,
     'mla_q_norm_2': 8.0,
     'mla_kv_norm_2': 7.249,
     'diff_subln_2': 12.447,
     'ffn_conv_b_2': 13.861,
     'norm_ffn_2': 5.307}
    for name, (base, spread) in spreads.items():
        noise = np.random.default_rng([zlib.crc32(name.encode()), seed]).standard_normal(out[name].shape)
        drawn = base * np.exp(spread * noise) if base else spread * noise
        out[name] = jnp.asarray(drawn.astype(out[name].dtype))
    for name, factor in factors.items():
        out[name] = (out[name] * factor).astype(out[name].dtype)
    return out
```

```python
import numpy as np
import concourse.bass as bass
from concourse import mybir
from concourse.alu_op_type import AluOpType as ALU

F32 = mybir.dt.float32
F32R = mybir.dt.float32r
I32 = mybir.dt.int32
ACT = mybir.ActivationFunctionType
AX = mybir.AxisListType

P = 128
D = 1024
KC = D // P
S = 256
T = 2 * S
FF = 2816
FC = FF // P
L1 = 2
HD = 64
NMOD = 9
EPS = 1e-6
NEG = -1e30
SLAB = KC * 2 * P
NBR_ROWS = 4
NBR_COLS = 64
NBR_DR = 2 * NBR_ROWS - 1
RPB_W = 31
SKEW = 128
CH = 64
NCH = S // CH
RH = 8
MH = 8
MN, MR = 64, 32
DH = 4
NBUCKET = 32
MAP_BYTES = 4 * (5 * 3 * P + DH * NBUCKET) + 4 * 3 * P + 64
LAMBDA_INIT = 0.8 - 0.6
MLA_SCALE = (MN + MR) ** -0.5
ROUND = 1.5 * 2.0 ** 23
TWO_PI = (6.28125, 0.0019350051879882812, float(2 * np.pi - 6.28125 - 0.0019350051879882812))

QCHUNKS = 8
KCHUNKS = 5
N_PROBS = 3


def head_at(c, s):
    if c < 3:
        return "win", 3 * s + c, 0, 64 * s
    if c < 5:
        return "glob", 2 * s + (c - 3), 1, 128 + 64 * s
    h = 2 * (c - 5) + s
    return "nbr", h, c - 3, 256 + 64 * h


def q_columns():
    base = {"win": 0, "glob": 6 * HD, "nbr": 10 * HD}
    cols = []
    for c in range(QCHUNKS):
        for s in range(2):
            g, h, _, _ = head_at(c, s)
            cols += [base[g] + h * HD + d for d in range(HD)]
    return cols


def kv_columns():
    a, b, n = 2 * HD, 2 * HD, 6 * HD
    o = D
    kw, vw = o, o + a
    kg, vg = o + 2 * a, o + 2 * a + b
    kn = o + 2 * a + 2 * b
    vn = kn + n
    k = [kw + i for i in range(a)] + [kg + i for i in range(b)] + [kn + i for i in range(n)]
    v = [vw + i for i in range(a)] + [vg + i for i in range(b)] + [vn + i for i in range(n)]
    return k, v


class Columns:
    def __init__(self):
        self.at, self.n = {}, 0

    def add(self, name, width):
        self.at[name] = self.n
        self.n += width


def vector_columns():
    v = Columns()
    for l in range(L1):
        v.add(("b_ada", l), NMOD * KC)
    for l in range(L1):
        for n in ("norm_ffn1", "norm_mix", "norm_ffn2"):
            v.add((n, l), KC)
        v.add(("q_gain", l), 1)
        v.add(("k_gain", l), 1)
        v.add(("sink", l), 6)
    v.add("norm_final", KC)
    v.add("c", KC)
    v.add("c_ctx", KC)
    v.add("norm_mix_2", KC)
    v.add("b_gate_2", 3 * KC)
    v.add("mu", 14)
    for n in ("w0", "a0", "k_k", "k_a", "r_k", "ln_w", "ln_b"):
        v.add(n, 4)
    v.add("mla_q_norm", 2)
    v.add("mla_kv_norm", 1)
    v.add("subln", 1)
    v.add("norm_ffn_2", KC)
    for j in range(3):
        v.add(("conv_w", j), 2 * FC)
    v.add("conv_b", 2 * FC)
    v.add("norm_final_2", KC)
    v.add("lambda", 4 * HD)
    v.add("rel_bias", NBUCKET * DH)
    return v


VC = vector_columns()


def const_columns():
    c = Columns()
    c.add("ident", P)
    c.add("ones", P)
    c.add("half_ones", P)
    c.add("swap", P)
    c.add("fold", 2)
    c.add("eps", 1)
    c.add("eps64", 1)
    c.add("gn_eps", 1)
    c.add("sub_eps", 1)
    c.add("inv_freq", 1)
    c.add("rope_sign", 1)
    c.kept = c.n
    c.add("cos", S)
    c.add("sin", S)
    c.add("win_mask", 2 * S)
    c.add("nbr_mask", NBR_COLS)
    c.add("causal", P)
    c.add("level", 6 * CH)
    c.add("strict", CH)
    c.add("incl", CH)
    c.add("ident64", CH)
    return c


CC = const_columns()


def constants():
    t = np.zeros((P, CC.n), np.float32)

    def put(name, a):
        a = np.asarray(a, np.float32)
        t[:, CC.at[name]:CC.at[name] + a.shape[1]] = a

    p = np.arange(P)
    put("ident", np.eye(P))
    put("ones", np.ones((P, P)))
    put("half_ones", (p[:, None] // 64 == p[None, :] // 64))
    put("swap", (p[:, None] == (p[None, :] ^ 32)))
    put("fold", np.stack([(p % 32 == s) for s in range(2)], 1))
    tok = np.arange(S)
    inv = (np.float32(10000.0) ** (-np.arange(16, dtype=np.float32) / np.float32(16))).astype(np.float32)
    ang = np.concatenate([(tok // 64).astype(np.float32)[:, None] * inv,
                          (tok % 64).astype(np.float32)[:, None] * inv], 1)
    put("cos", np.cos(ang).T[p % 32])
    put("sin", np.sin(ang).T[p % 32] * np.where(p % 64 < 32, -1.0, 1.0)[:, None])
    q = np.arange(2 * P).reshape(2, P)
    m = np.where(np.abs(q[:, :, None] - tok[None, None, :]) <= 128, 0.0, NEG)
    put("win_mask", m.transpose(1, 0, 2).reshape(P, 2 * S))
    c = p % 64
    start = np.clip(c - 8, 0, NBR_COLS - 16)[:, None]
    kc = np.arange(NBR_COLS)[None, :]
    put("nbr_mask", np.where((kc >= start) & (kc < start + 16), 0.0, NEG))
    put("causal", np.where(p[:, None] >= p[None, :], 0.0, NEG))
    s, tt = (p % CH)[:, None], np.arange(CH)[None, :]
    lev = [(tt // (2 << n) == s // (2 << n)) & (tt // (1 << n) > s // (1 << n)) for n in range(6)]
    put("level", np.concatenate(lev, 1))
    put("strict", s < tt)
    put("incl", s <= tt)
    put("ident64", s == tt)
    put("eps", np.full((P, 1), EPS))
    put("eps64", np.full((P, 1), HD * EPS))
    put("gn_eps", np.full((P, 1), 64e-5))
    put("sub_eps", np.full((P, 1), 1e-5))
    inv2 = (np.float32(10000.0) ** (-np.arange(0, MR, 2, dtype=np.float32) / np.float32(MR))).astype(np.float32)
    put("inv_freq", inv2[p % 16][:, None])
    put("rope_sign", np.where(p % 32 < 16, -1.0, 1.0)[:, None])
    return t


def bucket_starts():
    n = np.arange(0, 256)
    nf = np.maximum(n, 1).astype(np.float32)
    large = 16 + (np.log(nf / np.float32(16)) / np.float32(np.log(8.0)) * 16).astype(np.int32)
    b = np.where(n < 16, n, np.minimum(large, NBUCKET - 1))
    return [int(n[b >= k][0]) for k in range(1, NBUCKET)]


class Phase:
    def __init__(self, name, n, tiles, mod=False):
        self.name, self.n, self.tiles, self.mod = name, n, tiles, mod


ADA_TILES = 16
ADA_PANELS = 36
ADA_FIRST = 8


def phases():
    out = []
    for l in range(L1):
        m = l == 0
        out += [Phase(("up1", l), FC, 16, m), Phase(("down1", l), 16, 11, m), Phase(("in", l), 9, 16),
                Phase(("out", l), 4, 16, m), Phase(("up2", l), FC, 16, m), Phase(("down2", l), 16, 11)]
    out += [Phase("rwkv_in", 7, 16), Phase("gate_in", 12, 16), Phase("diff_in", 6, 16),
            Phase("mla_in", 2, 16), Phase("branch", 8, 12), Phase("w_o", 4, 16),
            Phase("up_2", FC, 16), Phase("down_2", 16, 11)]
    at = L1 * ADA_PANELS * P * ADA_TILES * P
    g, j = 0, ADA_FIRST
    for p in out:
        p.offset, p.first, p.first_ada = at, g, j
        at += p.n * P * p.tiles * P
        g += p.n
        j += p.n if p.mod else 0
    assert j == L1 * ADA_PANELS
    return out, at


PHASES, STREAM_SIZE = phases()
PHASE = {p.name: p for p in PHASES}


def panel_array(name, inp):
    def tiles(w, cols=None):
        w = np.asarray(w)
        if cols is not None:
            w = w[:, cols]
        k, n = w.shape
        return w.reshape(k // P, P, n // P, P).transpose(2, 1, 0, 3)

    def pairs(t):
        n, p, k, c = t.shape
        return t.reshape(n // 2, 2, p, k, c).transpose(0, 2, 1, 3, 4).reshape(n // 2, p, 2 * k, c)

    def wide(w, cols, width):
        w = np.asarray(w)[:, cols]
        n = w.shape[1] // width
        t = w.reshape(KC, P, n, width).transpose(2, 1, 0, 3)
        return t.reshape(n, P, KC * width // P, P)

    kind, l = name if isinstance(name, tuple) else (name, 0)
    if kind == "ada":
        return wide(inp["w_ada"][l], slice(None), 256)
    if kind in ("up1", "up2"):
        f = "ffn" + kind[2]
        return np.concatenate([tiles(inp[f"w_{f}_gate"][l]), tiles(inp[f"w_{f}_up"][l])], 2)
    if kind in ("down1", "down2"):
        t = tiles(inp[f"w_ffn{kind[4]}_down"][l])
        return t.reshape(KC, P, 2, 11, P).transpose(0, 2, 1, 3, 4).reshape(16, P, 11, P)
    if kind == "in":
        w = inp["w_in"][l]
        k, v = kv_columns()
        a = tiles(w, q_columns() + k)
        last = np.concatenate([a[12:13], wide(w, v[:128], 128)], 2)
        return np.concatenate([pairs(a[:12]), last, wide(w, v[128:], 256)], 0)
    if kind == "out":
        return pairs(tiles(np.asarray(inp["w_out"][l])[q_columns(), :]))
    w2 = np.asarray(inp["w_in_2"][0])
    rw, ml, df = 1792, 416, 1536
    if kind == "diff_in":
        o = rw + ml
        return np.concatenate([pairs(tiles(w2[:, o:o + 1024])), wide(w2, slice(o + 1024, o + 1536), 256)], 0)
    if kind == "mla_in":
        cq = pairs(tiles(w2[:, rw:rw + 256]))
        kr = [rw + 384 + i for i in range(32)]
        swapped = kr[16:] + kr[:16]
        return np.concatenate([cq, pairs(tiles(w2, [rw + 256 + i for i in range(128)]
                                               + kr + swapped + kr + swapped))], 0)
    if kind == "rwkv_in":
        return pairs(tiles(w2[:, :rw]))
    if kind == "gate_in":
        return pairs(tiles(w2[:, rw + ml + df:]))
    if kind == "branch":
        return np.concatenate([tiles(inp[f"w_branch_{b}_2"][0]) for b in ("rwkv", "mla", "diff")], 2)
    if kind == "w_o":
        return pairs(tiles(inp["w_o_2"][0]))
    if kind == "up_2":
        w = inp["ffn_w_up_2"][0]
        return np.concatenate([tiles(w[:, :FF]), tiles(w[:, FF:])], 2)
    if kind == "down_2":
        t = tiles(inp["ffn_w_down_2"][0])
        return t.reshape(KC, P, 2, 11, P).transpose(0, 2, 1, 3, 4).reshape(16, P, 11, P)
    raise KeyError(name)


def lay_out(inp):
    stream = np.empty(STREAM_SIZE, np.float32)
    for l in range(L1):
        a = panel_array(("ada", l), inp)
        stream[l * a.size:(l + 1) * a.size].reshape(a.shape)[...] = a
    for p in PHASES:
        a = panel_array(p.name, inp)
        assert a.shape == (p.n, P, p.tiles, P), (p.name, a.shape)
        stream[p.offset:p.offset + a.size].reshape(a.shape)[...] = a
    vec = np.zeros((P, VC.n), np.float32)

    def put(name, v, repeat=1):
        v = np.tile(np.asarray(v).reshape(-1), repeat).reshape(-1, P).T
        vec[:, VC.at[name]:VC.at[name] + v.shape[1]] = v

    def put_rows(name, v):
        v = np.asarray(v).reshape(1, -1)
        vec[:, VC.at[name]:VC.at[name] + v.shape[1]] = v

    for l in range(L1):
        put(("b_ada", l), inp["b_ada"][l])
        for n in ("norm_ffn1", "norm_mix", "norm_ffn2"):
            put((n, l), inp[n][l])
        put(("q_gain", l), inp["q_norm_glob"][l], 2)
        put(("k_gain", l), inp["k_norm_glob"][l], 2)
        put_rows(("sink", l), np.asarray(inp["sink_win"][l])[[3 * s + c for c in range(3) for s in range(2)]])
    for n in ("norm_final", "c", "c_ctx"):
        put(n, inp[n])
    for n, k in (("norm_mix_2", "norm_mix_2"), ("b_gate_2", "b_gate_2"), ("mu", "rwkv_mu_2"),
                 ("w0", "rwkv_w0_2"), ("a0", "rwkv_a0_2"), ("k_k", "rwkv_k_k_2"), ("k_a", "rwkv_k_a_2"),
                 ("r_k", "rwkv_r_k_2"), ("ln_w", "rwkv_ln_w_2"), ("ln_b", "rwkv_ln_b_2"),
                 ("mla_q_norm", "mla_q_norm_2"), ("mla_kv_norm", "mla_kv_norm_2"),
                 ("subln", "diff_subln_2"), ("norm_ffn_2", "norm_ffn_2"), ("conv_b", "ffn_conv_b_2"),
                 ("norm_final_2", "norm_final_2")):
        put(n, inp[k])
    for j in range(3):
        put(("conv_w", j), inp["ffn_conv_w_2"][0, j])
    put_rows("lambda", inp["diff_lambda_2"])
    put_rows("rel_bias", np.asarray(inp["rel_bias_2"]).T)

    def fm(x):
        x = np.asarray(x)
        return x.T.reshape(-1, P, x.shape[0]).transpose(1, 0, 2)

    uq = np.asarray(inp["mla_w_uq_2"][0]).reshape(2, P, MH, MN + MR).transpose(1, 0, 2, 3)
    half = MR // 2
    uq = np.concatenate([uq, uq[..., MN + half:], uq[..., MN:MN + half]], 3)
    ukv = np.asarray(inp["mla_w_ukv_2"][0]).reshape(P, MH, 2, MN).transpose(0, 2, 1, 3)
    small = np.concatenate([
        uq.reshape(P, -1), ukv.reshape(P, -1),
        np.concatenate([np.asarray(inp["rwkv_w2_2"][0]), np.asarray(inp["rwkv_a2_2"][0])], 0),
        np.asarray(inp["rwkv_g2_2"][0])], 1)
    pos = np.asarray(inp["positions_2"]).reshape(-1).astype(np.int32, copy=False)
    return {
        "stream": stream, "vec": vec, "const": constants(),
        "tokens": np.concatenate([fm(inp["x"][0]), fm(inp["ctx"][0])], 2),
        "rpb": np.ascontiguousarray(inp["rpb_nbr"]),
        "small": np.ascontiguousarray(small),
        "pos_row": np.ascontiguousarray(np.broadcast_to(pos, (P, S))),
        "pos_col": np.ascontiguousarray(pos.reshape(2, P).T),
    }


SM_UQ, SM_UKV = 0, 2 * MH * P
SM_WA = SM_UKV + 2 * MH * MN
SM_G = SM_WA + 512
SM_N = SM_G + 512


class Engine:

    def __init__(self, nc, queue, name):
        self.q, self.sem, self.n, self.seen = queue, nc.alloc_semaphore(name), 0, {}

    def after(self, *marks):
        for m in marks:
            if m is None:
                continue
            if isinstance(m, list):
                self.after(*m)
                continue
            sem, value = m
            if self.seen.get(sem.name, 0) < value:
                self.q.wait_ge(sem, value)
                self.seen[sem.name] = value

    def do(self, instruction):
        self.n += 1
        instruction.then_inc(self.sem, 1)
        return (self.sem, self.n)

    def last(self):
        return (self.sem, self.n) if self.n else None


class Count:

    def __init__(self, base, step=0, reg=None):
        self.base, self.step, self.reg = base, step, reg

    def plus(self, n):
        v = self.base + n
        return v if self.reg is None else self.reg * self.step + v

    def of(self, table):
        v = table[self.base]
        return v if self.reg is None else self.reg * (table[self.base + self.step] - v) + v

    def static(self):
        return self.reg is None

    def times(self, n):
        return Count(self.base * n, self.step * n, self.reg)


class Stream:

    def __init__(self, nc, e, source, buffers):
        self.nc, self.e, self.source = nc, e, source
        self.raw, self.hi, self.lo = buffers
        self.s_raw = [nc.alloc_semaphore(f"panel_loaded_{i}") for i in range(2)]
        self.s_hi = nc.alloc_semaphore("weights_hi_done")
        self.s_lo = nc.alloc_semaphore("weights_lo_done")
        self.s_ada = nc.alloc_semaphore("ada_panel_multiplied")
        self.s_pe = nc.alloc_semaphore("panel_multiplied")
        self.s_ev = nc.alloc_semaphore("group_evacuated")
        self.groups = 0
        self.used = PHASES
        self.slot, self.there, self.before = {}, {}, {}
        held, count = [None, None], [0, 0]

        def place(kind, n, slot):
            count[slot] += 16
            self.slot.setdefault(kind, []).append(slot)
            self.there.setdefault(kind, []).append(count[slot])
            self.before.setdefault(kind, []).append(held[slot])
            held[slot] = (self.s_ada if kind == "ada" else self.s_lo, n + 1)

        for j in range(ADA_FIRST):
            place("ada", j, j % 2)
        for ph in PHASES:
            for k in range(ph.n):
                place("own", ph.first + k, 0 if ph.mod else k % 2)
                if ph.mod:
                    place("ada", ph.first_ada + k, 1)

    def load(self, kind, n, k, offset, tiles):
        sp, size = self.nc.sync, P * tiles * P
        slot = self.slot[kind][n.base]
        before = self.before[kind][n.base]
        if before is not None:
            values = [b and b[1] for b in self.before[kind]]
            sp.wait_ge(before[0], n.of(values))
        at = k.times(size).plus(offset)
        sp.dma_start(self.raw[slot][:, 0:tiles * P], self.source[bass.ds(at, size)].rearrange("(p n) -> p n", p=P))\
            .then_inc(self.s_raw[slot], 16)

    def load_all(self):
        for j in range(2):
            self.load("ada", Count(j), Count(j), 0, ADA_TILES)
        with self.nc.sync.Fori(0, ADA_FIRST // 2 - 1) as i:
            for j in range(2):
                self.load("ada", Count(2 + j, 2, i), Count(2 + j, 2, i), 0, ADA_TILES)
        for ph in self.used:
            def panel(k):
                self.load("own", Count(ph.first + k.base, k.step, k.reg), k, ph.offset, ph.tiles)
                if ph.mod:
                    j = Count(ph.first_ada + k.base, k.step, k.reg)
                    self.load("ada", j, j, 0, ADA_TILES)

            loops = (ph.n - 2) // 2 if ph.n >= 6 else 0
            for k in range(2 if loops else ph.n):
                panel(Count(k))
            if loops:
                with self.nc.sync.Fori(0, loops) as i:
                    for k in range(2):
                        panel(Count(2 + k, 2, i))
                for k in range(2 + 2 * loops, ph.n):
                    panel(Count(k))

    def panels_done(self, name):
        return PHASE[name].first + PHASE[name].n

    def split(self, ph, j):
        a, v = self.e.A.q, self.e.V.q
        s = Count(ph.first + j.base, j.step, j.reg)
        raw, to, n = self.raw[self.slot["own"][s.base]], s.base % 2, ph.tiles * P
        a.wait_ge(self.s_raw[self.slot["own"][s.base]], s.of(self.there["own"]))
        if not s.static() or s.base >= 2:
            a.wait_ge(self.s_pe, s.plus(-1))
        a.activation(self.hi[to][:, 0:n], raw[:, 0:n], ACT.Copy).then_inc(self.s_hi, 1)
        v.wait_ge(self.s_hi, s.plus(1))
        v.tensor_tensor(self.lo[to][:, 0:n], raw[:, 0:n], self.hi[to][:, 0:n].bitcast(F32),
                        ALU.subtract).then_inc(self.s_lo, 1)

    def run(self, name, multiply, evacuate, finish=None, ppg=1, loop=True, second=None, third=None):
        ph = PHASE[name]
        k = PHASES.index(ph)
        after = self.used[k + 1] if k + 1 < len(self.used) else None
        pe = self.e.T.q
        n_groups = ph.n // ppg
        assert ph.n == n_groups * ppg
        g0 = self.groups

        def group(m):
            par = (g0 + m.base) % 2
            G = Count(g0 + m.base, m.step, m.reg)
            prev = Count(m.base - 1, m.step, m.reg)
            prevG = Count(G.base - 1, m.step, m.reg)
            prev2 = Count(m.base - 2, m.step, m.reg)
            lag2 = second and m.base >= 2
            done = Count(ph.first + m.base * ppg, m.step * ppg, m.reg)
            lag = not m.static() or m.base >= 1
            if lag2:
                second(prev2, par)
            if lag:
                evacuate(prev, 1 - par, prevG, done)
            if lag2:
                third(prev2, par)
            for part in range(ppg):
                nxt = Count(m.base * ppg + part + 1, m.step * ppg, m.reg)
                if not nxt.static() or nxt.base < ph.n:
                    self.split(ph, nxt)
                elif after is not None:
                    self.split(after, Count(0))
                panel = Count(ph.first + m.base * ppg + part, m.step * ppg, m.reg)
                if ph.mod:
                    j = Count(ph.first_ada + m.base * ppg + part, m.step * ppg, m.reg)
                    self.ada(j, lag or part > 0)
                pe.wait_ge(self.s_lo, panel.plus(1))
                if part == 0 and (not G.static() or G.base >= 2):
                    pe.wait_ge(self.s_ev, G.plus(-1))
                multiply(par, part, panel.base % 2).then_inc(self.s_pe, 1)
            if lag and finish:
                finish(prev, 1 - par, prevG)

        pairs = (n_groups - 4) // 2
        if loop and pairs >= 2:
            for m in range(2):
                group(Count(m))
            with self.nc.Fori(0, pairs, engines=[mybir.EngineType.PE, mybir.EngineType.Activation,
                                                 mybir.EngineType.DVE]) as i:
                for u in range(2):
                    group(Count(2 + u, 2, i))
            for m in range(2 + 2 * pairs, n_groups):
                group(Count(m))
        else:
            for m in range(n_groups):
                group(Count(m))
        if ph.mod:
            self.ada_last(ph.first_ada + ph.n - 1)
        m = n_groups - 1
        done = Count(ph.first + ph.n)
        if second:
            second(Count(m - 1), (g0 + m - 1) % 2)
        evacuate(Count(m), (g0 + m) % 2, Count(g0 + m), done)
        if second:
            third(Count(m - 1), (g0 + m - 1) % 2)
            second(Count(m), (g0 + m) % 2)
            third(Count(m), (g0 + m) % 2)
        if finish:
            finish(Count(m), (g0 + m) % 2, Count(g0 + m))
        self.groups += n_groups


def build(nc, ins, out):
    class e:
        pass
    e.T = Engine(nc, nc.tensor, "pe_done")
    e.A = Engine(nc, nc.scalar, "act_done")
    e.V = Engine(nc, nc.vector, "dve_done")
    e.G = Engine(nc, nc.gpsimd, "pool_done")
    pe, act, dve = e.T, e.A, e.V

    def sb(name, shape, dt=F32):
        return nc.alloc_sbuf_tensor(name, shape, dt)

    vec = sb("vec", [P, VC.n])
    const = sb("const", [P, CC.kept])
    raw = [sb(f"raw{i}", [P, SLAB]) for i in range(2)]
    whi = [sb(f"whi{i}", [P, SLAB], F32R) for i in range(2)]
    wlo = [sb(f"wlo{i}", [P, SLAB], F32R) for i in range(2)]
    H_AT = (nc.sbuf_base + 31) // 32 * 32
    h = sb("h", [P, KC, T])
    u_hi = sb("u_hi", [P, KC, T], F32R)
    u_lo = sb("u_lo", [P, KC, T], F32R)
    gates = nc.alloc_sbuf_tensor_at("gates", [P, 3 * KC, T], F32, offset=H_AT)[:, :, S:T]
    sil = [sb(f"sil{i}", [P, T]) for i in range(2)]
    prod = [sb(f"prod{i}", [P, T]) for i in range(2)]
    ssq = sb("ssq", [P, T])
    mod = sb("mod", [P, 2, L1 * NMOD * KC])
    mod_a = sb("mod_a", [P, L1, 3, 2, KC])
    mod_g = sb("mod_g", [P, L1, 3, 2, KC])
    arena_size = FC * T * 4 * 2
    ARENA_AT = (nc.sbuf_base + 31) // 32 * 32
    sb("arena", [P, arena_size // 4])
    banks = [nc.alloc_psum_tensor(f"bank{i}", [P, 512], F32) for i in range(8)]

    tables = [None]

    def cst(name, width=P, k=0):
        o = CC.at[name] + k
        if o >= CC.kept:
            return tables[0][:, o - CC.kept:o - CC.kept + width]
        return const[:, o:o + width]

    def vcol(name, k=0, width=1):
        o = VC.at[name] + k
        return vec[:, o:o + width]

    class Arena:

        def __init__(self):
            self.at = 0

        def new(self, name, shape, dt=F32):
            size = int(np.prod(shape[1:])) * 4
            t = nc.alloc_sbuf_tensor_at(name, shape, dt, offset=ARENA_AT + self.at)
            self.at += (size + 31) // 32 * 32
            assert self.at <= arena_size, (name, self.at, arena_size)
            return t

    s_in = nc.alloc_semaphore("small_inputs_loaded")
    sp = nc.sync
    sp.dma_start(vec[:, :], ins["vec"]).then_inc(s_in, 16)
    sp.dma_start(const[:, :], ins["const"][:, 0:CC.kept]).then_inc(s_in, 16)
    sp.dma_start(h[:, :, :], ins["tokens"]).then_inc(s_in, 16)
    loaded = (s_in, 48)

    s_rpb = nc.alloc_semaphore("rpb_moved")
    rows = L1 * 6 * NBR_DR
    skew = nc.dram_tensor("skew", [(NBR_COLS + 1) * rows * SKEW], F32, kind="Internal").ap()
    pool = e.G
    ar = Arena()
    stage = [ar.new(f"rpb_stage{l}", [NBR_COLS, rows // L1, SKEW]) for l in range(L1)]
    pad = (SKEW - 2) // 2 + 1 - RPB_W // 2 - 1
    zeroed = [pool.do(pool.q.memset(stage[l][:, :, :], 0.0)) for l in range(L1)]
    n_rpb = 0
    for l in range(L1):
        pool.after(zeroed[l])
        for hh in range(6):
            src = ins["rpb"][l, hh, 7 - (NBR_ROWS - 1):7 + NBR_ROWS, :]
            src = src.rearrange("(o r) w -> o r w", o=1).to_broadcast([NBR_COLS, NBR_DR, RPB_W])
            pool.q.dma_start(stage[l][:, hh * NBR_DR:(hh + 1) * NBR_DR, pad:pad + RPB_W], src).then_inc(s_rpb, 16)
            n_rpb += 16
    pool.q.wait_ge(s_rpb, n_rpb)
    flat = skew[0:NBR_COLS * rows * SKEW].rearrange("(c l n) -> c l n", c=NBR_COLS, l=L1)
    for l in range(L1):
        pool.q.dma_start(flat[:, l, :], stage[l][:, :, :].rearrange("p a b -> p (a b)")).then_inc(s_rpb, 16)
        n_rpb += 16
    rpb_in_dram = (s_rpb, n_rpb)
    pool.q.wait_ge(s_rpb, n_rpb)
    stage_free = pool.do(pool.q.memset(ssq[:, :], 0.0))

    csil = sb("csil", [P, KC, 32])
    cz = dve.do(dve.q.memset(csil[:, :, :], 0.0))
    act.after(loaded, cz)
    act.do(act.q.activation(csil[:, :, 0], vcol("c", 0, KC), ACT.Silu))
    c_ready = act.do(act.q.activation(csil[:, :, 1], vcol("c_ctx", 0, KC), ACT.Silu))

    st = Stream(nc, e, ins["stream"], (raw, whi, wlo))
    st.load_all()
    s_row = nc.alloc_semaphore("mod_rows_copied")
    s_fold = nc.alloc_semaphore("mod_rows_folded")
    s_mod = nc.alloc_semaphore("mod_biased")
    inv = sb("inv_norm", [P, T // P])
    diag = sb("inv_norm_diagonal", [P, T])
    row = [diag[:, 256 * i:256 * i + 256] for i in range(2)]
    ada_done = [0]

    def ada_fold(j):
        par = j.base % 2
        pe.q.wait_ge(s_row, j.plus(1))
        if not j.static() or j.base >= 2:
            pe.q.wait_ge(s_mod, j.plus(-1))
        for c in range(2):
            x = pe.q.matmul(banks[4 + par][:, 2 * c:2 * c + 2], row[par][:, c * P:(c + 1) * P], cst("fold", 2),
                            start=True, stop=True)
        x.then_inc(s_fold, 1)
        dve.q.wait_ge(s_fold, j.plus(1))
        at_ = j.times(2).plus(0)
        bias = vec[:, bass.ds(at_ + VC.at[("b_ada", 0)], 2)].rearrange("p (s c) -> p s c", s=1)
        dve.q.tensor_tensor(mod[:, :, bass.ds(at_, 2)], banks[4 + par][:, 0:4].rearrange("p (c s) -> p s c", s=2),
                            bias.to_broadcast([P, 2, 2]), ALU.add).then_inc(s_mod, 1)

    def ada_panel(j, fold=True):
        par = j.base % 2
        slot = st.slot["ada"][j.base]
        pe.q.wait_ge(st.s_raw[slot], j.of(st.there["ada"]))
        if not j.static() or j.base >= 2:
            pe.q.wait_ge(s_row, j.plus(-1))
        for r in range(2):
            for q in range(4):
                kc = 4 * r + q
                x = pe.q.matmul(banks[6 + par][32 * q:32 * q + 32, 0:256], csil[:, kc, :],
                                raw[slot][:, kc * 256:(kc + 1) * 256], start=(r == 0), stop=(r == 1))
        x.then_inc(st.s_ada, 1)
        if fold:
            ada_fold(Count(j.base - 1, j.step, j.reg))
        dve.q.wait_ge(st.s_ada, j.plus(1))
        if not j.static() or j.base >= 2:
            dve.q.wait_ge(s_fold, j.plus(-1))
        dve.q.tensor_copy(row[par], banks[6 + par][:, 0:256]).then_inc(s_row, 1)

    def ada_last(j):
        ada_fold(Count(j))
        ada_done[0] = j + 1
        pe.after((s_mod, j + 1))

    st.ada, st.ada_last = ada_panel, ada_last
    pe.after(loaded, c_ready)
    dve.after(loaded)
    ada_panel(Count(0), False)
    ada_panel(Count(1))
    with nc.Fori(0, ADA_FIRST // 2 - 1, engines=[mybir.EngineType.PE, mybir.EngineType.DVE]) as i:
        for j in range(2):
            ada_panel(Count(2 + j, 2, i))
    ada_last(ADA_FIRST - 1)
    mods_ready = [None]

    def mod_part(l, x, s):
        o = (l * NMOD + x) * KC
        return mod[:, s, o:o + KC]

    def mod_scales(l, n):
        dve.after((s_mod, ada_done[0]))
        for s in range(2):
            name = ("norm_ffn1", "norm_mix", "norm_ffn2")[n]
            mods_ready[0] = dve.do(dve.q.scalar_tensor_tensor(
                out=mod_a[:, l, n, s, :], in0=mod_part(l, 3 * n + 1, s), scalar=1.0, in1=vcol((name, l), 0, KC),
                op0=ALU.add, op1=ALU.mult))

    def mod_gates(l, n):
        dve.after((s_mod, ada_done[0]))
        for s in range(2):
            mods_ready[0] = dve.do(dve.q.tensor_scalar(mod_g[:, l, n, s, :], mod_part(l, 3 * n + 2, s),
                                                       1.0 if n == 1 else 0.5, None, ALU.mult))
        dve.after(mods_ready[0])

    mod_scales(0, 0)

    s_sq = nc.alloc_semaphore("square_done")
    s_ss = nc.alloc_semaphore("square_added")
    sq_count = [0]
    act.after(loaded, stage_free)
    dve.after(stage_free)

    def add_square(c, n, ready=None, count=None):
        k = count or Count(sq_count[0])
        par = k.base % 2
        if not k.static() or k.base >= 2:
            act.q.wait_ge(s_ss, k.plus(-1))
        src = h[:, c, 0:n] if isinstance(c, int) else h[:, c, 0:n]
        act.q.activation(prod[par][:, 0:n], src, ACT.Square).then_inc(s_sq, 1)
        dve.q.wait_ge(s_sq, k.plus(1))
        if not k.static() or k.base >= 1:
            dve.q.wait_ge(s_ss, k.plus(0))
        dve.q.tensor_tensor(ssq[:, 0:n], ssq[:, 0:n], prod[par][:, 0:n], ALU.add).then_inc(s_ss, 1)
        if count is None:
            sq_count[0] += 1

    for c in range(KC):
        add_square(c, T)

    def norm_scale(n, eps="eps"):
        nt = n // P
        pe.after((s_ss, sq_count[0]), loaded)
        for t in range(nt):
            m = pe.q.matmul(banks[5][:, t:t + 1], ssq[:, t * P:(t + 1) * P], cst("ones", 1), start=True, stop=True)
        m = pe.do(m)
        act.after(m)
        r = act.do(act.q.activation(inv[:, 0:nt], banks[5][:, 0:nt], ACT.Sqrt, bias=cst(eps, 1), scale=1.0 / D))
        dve.after(r)
        r = dve.do(dve.q.reciprocal(inv[:, 0:nt], inv[:, 0:nt]))
        dve.after(r)
        for t in range(nt):
            r = dve.do(dve.q.tensor_scalar(diag[:, t * P:(t + 1) * P], cst("ident"), inv[:, t:t + 1], None, ALU.mult))
        pe.after(r)
        return pe.do(pe.q.matmul(banks[4][:, 0:n], cst("ones"), diag[:, 0:n], start=True, stop=True))

    def clear_squares(n):
        z = dve.do(dve.q.memset(ssq[:, 0:n], 0.0))
        dve.after(z)

    def root_table():
        act.do(act.q.activation(root_warm[:, :], cst("eps", 1), ACT.Sqrt))

    root_warm = sb("root_warm", [P, 1])
    tmp_free = [None, None]

    def norm(streams, coeff):
        n = streams * S
        rd = norm_scale(n)
        dve.after(rd, mods_ready[0])
        act.after(mods_ready[0])
        marks = [None] * KC
        hi = [None] * KC

        def lo_part(c):
            dve.after(hi[c])
            marks[c] = dve.do(dve.q.tensor_tensor(u_lo[:, c, 0:n], sil[c % 2][:, 0:n],
                                                  u_hi[:, c, 0:n].bitcast(F32), ALU.subtract))

        for c in range(KC):
            par = c % 2
            dve.after(tmp_free[par])
            a = dve.do(dve.q.tensor_tensor(prod[par][:, 0:n], h[:, c, 0:n], banks[4][:, 0:n], ALU.mult))
            act.after(a, marks[c - 2] if c >= 2 else None)
            for s in range(streams):
                A, B = coeff(c, s)
                b = act.do(act.q.activation(sil[par][:, s * S:(s + 1) * S], prod[par][:, s * S:(s + 1) * S],
                                            ACT.Identity, scale=A, bias=B if B is not None else 0.0))
            tmp_free[par] = b
            act.after(b)
            hi[c] = act.do(act.q.activation(u_hi[:, c, 0:n], sil[par][:, 0:n], ACT.Copy))
            if c >= 1:
                lo_part(c - 1)
        lo_part(KC - 1)
        clear_squares(n)
        return marks

    def mod_coeff(l, n):
        return lambda c, s: (mod_a[:, l, n, s, c:c + 1], mod_part(l, 3 * n, s)[:, c:c + 1])

    def three(dst, w, x, start, stop):
        pe.q.matmul(dst, w[0], x[0], start=start, stop=False)
        pe.q.matmul(dst, w[0], x[1], start=False, stop=False)
        return pe.q.matmul(dst, w[1], x[0], start=False, stop=stop)

    def pair_products(par, slot, x, n, ready=None):
        if ready is None:
            for b in range(2):
                for kc in range(KC):
                    r = three(banks[2 * par + b][:, 0:n], tile_of(slot, b * KC + kc), chunk_of(x, kc, 0, n),
                              kc == 0, kc == KC - 1)
            return r
        for kc in range(KC):
            pe.after(ready[kc])
            for b in range(2):
                r = three(banks[2 * par + b][:, 0:n], tile_of(slot, b * KC + kc), chunk_of(x, kc, 0, n),
                          kc == 0, kc == KC - 1)
        return r

    def tile_of(slot, t, width=P):
        return (whi[slot][:, t * P:t * P + width], wlo[slot][:, t * P:t * P + width])

    def chunk_of(pair, c, lo, hi):
        return (pair[0][:, c, lo:hi], pair[1][:, c, lo:hi])

    u = (u_hi, u_lo)
    s_sil = nc.alloc_semaphore("gate_activated")
    s_hh = nc.alloc_semaphore("hidden_hi_done")
    s_hl = nc.alloc_semaphore("hidden_lo_done")
    hidden_count = [0]
    far = Arena()
    hidden = [far.new(f"hidden_{n}", [P, FC, T], F32R) for n in ("hi", "lo")]
    far.at = 0
    hidden_s = [far.new(f"hidden_x_{n}", [P, FC, S], F32R) for n in ("hi", "lo")]

    def at(m):
        return m.plus(0)

    def finish_hidden(n, dst, sq0):
        def finish(m, par, G):
            k = Count(sq0 + m.base, m.step, m.reg)
            act.q.wait_ge(st.s_ev, G.plus(1))
            act.q.activation(dst[0][:, at(m), 0:n], prod[par][:, 0:n], ACT.Copy).then_inc(s_hh, 1)
            dve.q.wait_ge(s_hh, k.plus(1))
            dve.q.tensor_tensor(dst[1][:, at(m), 0:n], prod[par][:, 0:n],
                                dst[0][:, at(m), 0:n].bitcast(F32), ALU.subtract).then_inc(s_hl, 1)
        return finish

    def gate_up(name, n, ready, x, hidden):
        h0 = hidden_count[0]
        first = [ready]

        def multiply(par, part, slot):
            return pair_products(par, slot, x, n, first.pop() if first else None)

        def evacuate(m, par, G, done):
            k = Count(h0 + m.base, m.step, m.reg)
            act.q.wait_ge(st.s_pe, at(done))
            if not G.static() or G.base >= 2:
                act.q.wait_ge(st.s_ev, G.plus(-1))
            act.q.activation(sil[par][:, 0:n], banks[2 * par][:, 0:n], ACT.Silu).then_inc(s_sil, 1)
            dve.q.wait_ge(s_sil, k.plus(1))
            if not k.static() or k.base >= 2:
                dve.q.wait_ge(s_hh, k.plus(-1))
            dve.q.tensor_tensor(prod[par][:, 0:n], sil[par][:, 0:n], banks[2 * par + 1][:, 0:n],
                                ALU.mult).then_inc(st.s_ev, 1)

        st.run(name, multiply, evacuate, finish_hidden(n, hidden, h0))
        hidden_count[0] += FC

    def down(name, n, gates, hidden):
        q0 = sq_count[0]
        root_table()
        pe.after((s_hl, hidden_count[0]))

        def multiply(par, part, slot):
            for t in range(11):
                kc = part * 11 + t
                r = three(banks[2 * par][:, 0:n], tile_of(slot, t), chunk_of(hidden, kc, 0, n),
                          kc == 0, kc == FC - 1)
            return r

        def evacuate(m, par, G, done):
            dve.q.wait_ge(st.s_pe, at(done))
            residual(at(m), banks[2 * par], n, lambda s: gates(m, s)).then_inc(st.s_ev, 1)
            act.q.wait_ge(st.s_ev, G.plus(1))
            add_square(at(m), n, count=Count(q0 + m.base, m.step, m.reg))

        st.run(name, multiply, evacuate, ppg=2)
        sq_count[0] += KC

    def residual(m, bank, n, gate, off=0):
        for s in range(n // S):
            lo, hi = s * S, (s + 1) * S
            r = dve.q.scalar_tensor_tensor(out=h[:, m, lo:hi], in0=bank[:, lo:hi], scalar=gate(s),
                                           in1=h[:, m, lo:hi], op0=ALU.mult, op1=ALU.add)
        return r

    def mod_gate(l, n):
        def gate(m, s):
            if m.static():
                return mod_g[:, l, n, s, m.base:m.base + 1]
            return mod_g[:, l, n, s, bass.ds(m.plus(0), 1)]
        return gate

    top = Arena()
    top.at = arena_size - MAP_BYTES
    rel = top.new("rel_bias_map", [P, DH, 3 * P])
    dist = top.new("distance", [P, 3 * P])
    bucket = top.new("bucket_step", [P, 3 * P])
    steps = top.new("bucket_steps", [P, DH, NBUCKET])
    pcol = top.new("pos_col", [P, 2], I32)
    pcolf = top.new("pos_col_f", [P, 2])
    top.at = arena_size - MAP_BYTES
    prow = top.new("pos_row", [P, S], I32)

    def bias_map():
        s_pos = nc.alloc_semaphore("positions_loaded")
        pool.after(loaded, pool.last())
        pool.q.dma_start(prow[:, :], ins["pos_row"]).then_inc(s_pos, 16)
        pool.q.dma_start(pcol[:, :], ins["pos_col"]).then_inc(s_pos, 16)
        pool.after((s_pos, 32))
        table = vcol("rel_bias", 0, NBUCKET * DH).rearrange("p (h b) -> p h b", h=DH)
        pool.after(pool.do(pool.q.tensor_copy(bucket[:, 0:S], prow[:, :])))
        pool.after(pool.do(pool.q.tensor_copy(pcolf[:, :], pcol[:, :])))
        z = pool.do(pool.q.tensor_tensor(steps[:, :, 1:NBUCKET], table[:, :, 1:NBUCKET], table[:, :, 0:NBUCKET - 1],
                                     ALU.subtract))
        for qt in range(2):
            w = (qt + 1) * P
            pool.after(z)
            z = pool.do(pool.q.tensor_scalar(dist[:, qt * P:qt * P + w], bucket[:, 0:w], pcolf[:, qt:qt + 1], -1.0,
                                             ALU.subtract, ALU.mult))
        pool.after(z)
        for hh in range(DH):
            pool.after(z)
            z = pool.do(pool.q.tensor_scalar(rel[:, hh, :], dist[:, :], 0.0, table[:, hh, 0:1], ALU.mult, ALU.add))
        for b, start in enumerate(bucket_starts()):
            for hh in range(DH):
                pool.after(z)
                z = pool.do(pool.q.tensor_scalar(bucket[:, :], dist[:, :], float(start), steps[:, hh, b + 1:b + 2],
                                                 ALU.is_ge, ALU.mult))
                pool.after(z)
                z = pool.do(pool.q.tensor_tensor(rel[:, hh, :], rel[:, hh, :], bucket[:, :], ALU.add))
        return z

    for l in range(L1):
        last = l == L1 - 1
        if l == 0:
            st.split(PHASES[0], Count(0))
        ready = norm(2, mod_coeff(l, 0))
        gate_up(("up1", l), T, ready, u, hidden)
        if l == 0:
            mod_gates(0, 0)
            mod_scales(0, 1)
            mod_gates(0, 1)
        down(("down1", l), T, mod_gate(l, 0), hidden)

        if l == 0:
            mod_scales(0, 2)
            mod_gates(0, 2)
        ready = norm(2, mod_coeff(l, 1))
        qn = S if last else T
        ar = Arena()
        qT = ar.new(f"qT{l}", [P, QCHUNKS, T])
        kT = ar.new(f"kT{l}", [P, KCHUNKS, T])
        vt = ar.new(f"v{l}", [P, 4, 5 * P])
        tab = ar.new(f"tables{l}", [P, CC.n - CC.kept])
        nbr = ar.new(f"nbr_bias{l}", [P, 6, NBR_DR + 1, NBR_COLS])
        pbuf = [ar.new(f"probs{l}_{i}", [P, T]) for i in range(N_PROBS)]
        ptb = [[ar.new(f"probs_t{l}_{i}_{s}", [P, 4, S]) for s in range(2)] for i in range(2)]
        tables[0] = tab

        pool.after((st.s_pe, PHASE[("down1", l)].first + 16))
        s_tab = nc.alloc_semaphore(f"tables_loaded{l}")
        pool.q.dma_start(tab[:, :], ins["const"][:, CC.kept:CC.n]).then_inc(s_tab, 16)
        pool.q.wait_ge(*rpb_in_dram)
        z = [pool.do(pool.q.memset(nbr[0:64, :, NBR_DR, :], 0.0)),
             pool.do(pool.q.memset(nbr[64:128, :, 0, :], 0.0))]
        pitch = rows * SKEW - 1
        n_tab = 16
        for half in range(2):
            for hh in range(6):
                o = (l * 6 + hh) * NBR_DR * SKEW + NBR_COLS - 1
                src = skew[o:o + NBR_COLS * pitch].rearrange("(c n) -> c n", n=pitch)[:, 0:NBR_DR * SKEW]
                src = src.rearrange("c (r j) -> c r j", j=SKEW)[:, :, 0:NBR_COLS]
                dst = nbr[64 * half:64 * half + 64, hh, half:half + NBR_DR, :]
                pool.q.dma_start(dst, src).then_inc(s_tab, 16)
                n_tab += 16
        tab_ready = (s_tab, n_tab)
        if last:
            map_ready = bias_map()
        dve.after(tab_ready, z)
        mask_rows = cst("nbr_mask", NBR_COLS).rearrange("p (o c) -> p o c", o=1).to_broadcast([P, NBR_DR + 1, NBR_COLS])
        for hh in range(6):
            nbr_ready = dve.do(dve.q.tensor_tensor(nbr[:, hh, :, :], nbr[:, hh, :, :], mask_rows, ALU.add))

        first = [ready]
        kinds = [(("q", 2 * i), ("q", 2 * i + 1)) for i in range(4)] + \
                [(("k", 0), ("k", 1)), (("k", 2), ("k", 3)), (("k", 4), ("v", 0))] + \
                [(("v", P), ("v", P)), (("v", 3 * P), ("v", 3 * P))]
        step = [0]

        def multiply(par, part, slot):
            pair = kinds[step[0]]
            step[0] += 1
            if pair[0][0] == "v":
                for t in range(4):
                    for kc in range(KC):
                        w = (whi[slot][:, kc * 256:(kc + 1) * 256], wlo[slot][:, kc * 256:(kc + 1) * 256])
                        r = three(banks[2 * par + t // 2][:, 256 * (t % 2):256 * (t % 2) + 256],
                                  chunk_of(u, kc, t * P, t * P + P), w, kc == 0, kc == KC - 1)
                return r
            if pair[1][0] == "q":
                return pair_products(par, slot, u, qn, first.pop() if first else None)
            for b, (kind, c) in enumerate(pair):
                n = qn if kind == "q" else T
                if kind != "v":
                    for kc in range(KC):
                        r = three(banks[2 * par + b][:, 0:n], tile_of(slot, b * KC + kc),
                                  chunk_of(u, kc, 0, n), kc == 0, kc == KC - 1)
                    continue
                for t in range(4):
                    for kc in range(KC):
                        r = three(banks[2 * par + b][:, P * t:P * t + P], chunk_of(u, kc, t * P, t * P + P),
                                  tile_of(slot, KC + kc), kc == 0, kc == KC - 1)
            return r

        def evacuate(m, par, G, done):
            act.q.wait_ge(st.s_pe, at(done))
            for b, (kind, c) in enumerate(kinds[m.base]):
                src = banks[2 * par + b]
                if kind == "q":
                    r = act.q.activation(qT[:, c, 0:qn], src[:, 0:qn], ACT.Copy,
                                         scale=1.0 if c in (3, 4) else HD ** -0.5)
                elif kind == "k":
                    r = act.q.activation(kT[:, c, :], src[:, :], ACT.Copy)
                elif c == 0:
                    r = act.q.activation(vt[:, :, 0:P], src[:, :].rearrange("p (t c) -> p t c", t=4), ACT.Copy)
                else:
                    r = act.q.activation(vt[:, 2 * b:2 * b + 2, c:c + 256],
                                         src[:, :].rearrange("p (t c) -> p t c", t=2), ACT.Copy)
            r.then_inc(st.s_ev, 1)

        st.run(("in", l), multiply, evacuate, loop=False)
        projected = (st.s_ev, st.groups)

        act.after(projected)
        dve.after(projected)
        pe.after(projected, tab_ready)
        places = [(kT, 1, T, "k_gain", prod[0]), (qT, 3, qn, "q_gain", prod[1]), (qT, 4, qn, "q_gain", sil[0])]
        roots = {}
        for i, (t, c, n, gain, root) in enumerate(places):
            pe.after(act.do(act.q.activation(root[:, 0:n], t[:, c, 0:n], ACT.Square)))
            roots[i] = pe.do(pe.q.matmul(banks[5 + i][:, 0:n], cst("half_ones"), root[:, 0:n], start=True, stop=True))
        for i, (t, c, n, gain, root) in enumerate(places):
            act.after(roots[i])
            isq = gain == "q_gain"
            roots[i] = act.do(act.q.activation(root[:, 0:n], banks[5 + i][:, 0:n], ACT.Sqrt,
                                               bias=cst("eps64" if isq else "eps", 1), scale=1.0 if isq else 1.0 / HD))
        pe.after(roots[2])
        normed, prepared, turned = {}, {}, {}

        def norm_step(i, half):
            t, c, _, gain, root = places[i]
            cols = slice(half * S, half * S + S)
            dve.after(roots[i])
            dve.after(dve.do(dve.q.reciprocal(root[:, cols], root[:, cols])))
            normed[(t.name, c)] = dve.do(dve.q.scalar_tensor_tensor(
                out=t[:, c, cols], in0=t[:, c, cols], scalar=vcol((gain, l)), in1=root[:, cols],
                op0=ALU.mult, op1=ALU.mult))

        def swap_step(t, c):
            pe.after(normed.get((t.name, c)), turned.get("read"))
            turned["swap"] = pe.do(pe.q.matmul(banks[5][:, 0:S], cst("swap"), t[:, c, 0:S], start=True, stop=True))

        def turn_step(t, c):
            tmp = sil[1][:, 0:S]
            dve.after(turned["swap"])
            m1 = turned["read"] = dve.do(dve.q.tensor_tensor(tmp, banks[5][:, 0:S], cst("sin", S), ALU.mult))
            m2 = dve.do(dve.q.tensor_tensor(t[:, c, 0:S], t[:, c, 0:S], cst("cos", S), ALU.mult))
            dve.after(m1, m2)
            prepared[(t.name, c)] = dve.do(dve.q.tensor_tensor(t[:, c, 0:S], t[:, c, 0:S], tmp, ALU.add))

        steps_ = [(swap_step, turn_step, (t, c)) for t, c in ((kT, 0), (qT, 0), (qT, 1), (qT, 2))]
        steps_ += [(None, norm_step, (i, half)) for i, p in enumerate(places) for half in range(p[2] // S)]
        steps_ += [(swap_step, turn_step, (t, c)) for t, c in ((kT, 1), (qT, 3), (qT, 4))]
        queue = steps_[:]
        waiting = []

        def prepare_step():
            if waiting:
                waiting.pop()()
            if queue:
                first_, then, args = queue.pop(0)
                if first_:
                    first_(*args)
                waiting.append(lambda: then(*args))

        units = []
        for c in (5, 6, 7, 0, 1, 2, 3, 4):
            for stream in range(1 if last else 2):
                for qt in range(2):
                    for s in range(2):
                        units.append((c, s, stream, qt))
        dve.after(nbr_ready)
        neg_sink = sb(f"neg_sink{l}", [P, 6])
        dve.after(loaded)
        sink_ready = dve.do(dve.q.tensor_scalar(neg_sink[:, :], vcol(("sink", l), 0, 6), -1.0, None, ALU.mult))
        stat = sb(f"stat{l}", [P, 6, 4])
        marks = [dict() for _ in units]
        score_banks = banks[2:5]
        quads_done = {}

        def scores(i):
            c, s, stream, qt = units[i]
            _, _, kc, _ = head_at(c, s)
            rows_ = slice(64 * s, 64 * s + 64)
            o = stream * S + qt * P
            key0 = stream * S
            if i >= 3:
                pe.after(marks[i - 3]["exp"])
            if c < 5:
                pe.after(prepared[(qT.name, c)], prepared[(kT.name, kc)])
            marks[i]["scores"] = pe.do(pe.q.matmul(score_banks[i % 3][:, 0:T - key0], qT[rows_, c, o:o + P],
                                                   kT[rows_, kc, key0:T], start=True, stop=True))

        def exponentials(i):
            c, s, stream, qt = units[i]
            kind, head, _, _ = head_at(c, s)
            nk = T - stream * S
            b = score_banks[i % 3]
            k = i % 6
            m = marks[i]
            dve.after(m["scores"])
            bias = None
            if stream == 0 and kind == "win":
                bias, left = cst("win_mask", S, qt * S), b[:, 0:S]
            if stream == 0 and kind == "nbr":
                first = NBR_DR - NBR_ROWS - 2 * qt
                bias, left = nbr[:, head, first:first + NBR_ROWS, :], b[:, 0:S].rearrange("p (r c) -> p r c", r=NBR_ROWS)
            if bias is not None:
                dve.after(dve.do(dve.q.tensor_tensor(left, left, bias, ALU.add)))
            mx = dve.do(dve.q.tensor_reduce(out=stat[:, k, 0:1], in_=b[:, 0:nk], axis=AX.X, op=ALU.max, negate=True))
            if kind == "win":
                dve.after(mx, sink_ready)
                j = 2 * c + s
                mx = dve.do(dve.q.tensor_tensor(stat[:, k, 0:1], stat[:, k, 0:1], neg_sink[:, j:j + 1], ALU.min))
            act.after(mx, marks[i - N_PROBS].get("transposed") if i >= N_PROBS else None)
            m["exp"] = act.do(act.q.activation(pbuf[i % N_PROBS][:, 0:nk], b[:, 0:nk], ACT.Exp, bias=stat[:, k, 0:1],
                                               accum_out=stat[:, k, 1:2]))
            if kind == "win":
                m["sink"] = act.do(act.q.activation(stat[:, k, 2:3], vcol(("sink", l), j), ACT.Exp, bias=stat[:, k, 0:1]))

        def normalise(i):
            c, s, stream, qt = units[i]
            nk = T - stream * S
            k = i % 6
            m = marks[i]
            dve.after(m["exp"], m.get("sink"))
            if "sink" in m:
                dve.after(dve.do(dve.q.tensor_tensor(stat[:, k, 1:2], stat[:, k, 1:2], stat[:, k, 2:3], ALU.add)))
            dve.after(dve.do(dve.q.reciprocal(stat[:, k, 3:4], stat[:, k, 1:2])))
            pb = pbuf[i % N_PROBS][:, 0:nk]
            m["norm"] = dve.do(dve.q.tensor_scalar(pb, pb, stat[:, k, 3:4], None, ALU.mult))

        def transposes(i):
            c, s, stream, qt = units[i]
            nt = 4 - 2 * stream
            m = marks[i]
            pe.after(m["norm"], marks[i - 2].get("copied") if i >= 2 else None)
            for t in range(nt):
                r = pe.q.transpose(banks[6 + i % 2][:, t * P:(t + 1) * P], pbuf[i % N_PROBS][:, t * P:(t + 1) * P],
                                   cst("ident"))
            m["transposed"] = pe.do(r)
            quad = i // 4
            act.after(m["transposed"], quads_done.get(quad - 2))
            m["copied"] = act.do(act.q.activation(ptb[quad % 2][s][:, 0:nt, qt * P:(qt + 1) * P],
                                                  banks[6 + i % 2][:, 0:nt * P].rearrange("p (t q) -> p t q", t=nt),
                                                  ACT.Copy))

        def values(i):
            if i % 4 != 3:
                return
            c, _, stream, _ = units[i]
            nt = 4 - 2 * stream
            quad = i // 4
            b = banks[quad % 2]
            pe.after(marks[i]["copied"], quads_done.get(quad - 2))
            for t in range(nt):
                for s in range(2):
                    vo = head_at(c, s)[3]
                    r = pe.q.matmul(b[64 * s:64 * s + 64, 0:S], vt[:, t + 2 * stream, vo:vo + HD],
                                    ptb[quad % 2][s][:, t, :], start=(t == 0), stop=(t == nt - 1))
            marks[i]["pv"] = pe.do(r)

        def split_y(i):
            if i % 4 != 3:
                return
            c, _, stream, _ = units[i]
            b = banks[(i // 4) % 2]
            col = slice(stream * S, stream * S + S)
            act.after(marks[i]["pv"])
            hi = act.do(act.q.activation(u_hi[:, c, col], b[:, 0:S], ACT.Copy))
            dve.after(hi)
            quads_done[i // 4] = dve.do(dve.q.tensor_tensor(u_lo[:, c, col], b[:, 0:S], u_hi[:, c, col].bitcast(F32),
                                                            ALU.subtract))

        scores(0)
        scores(1)
        for i in range(len(units) + 4):
            if i + 2 < len(units):
                scores(i + 2)
            if i < len(units):
                exponentials(i)
            if 1 <= i <= len(units):
                normalise(i - 1)
            if 2 <= i < len(units) + 2:
                transposes(i - 2)
            if 3 <= i < len(units) + 3:
                values(i - 3)
            if i >= 4:
                split_y(i - 4)
            prepare_step()
        y_ready = [quads_done[len(units) // 4 - 1]]

        hn = qn
        root_table()

        def multiply(par, part, slot):
            return pair_products(par, slot, u, hn)

        def evacuate(m, par, G, done):
            dve.q.wait_ge(st.s_pe, at(done))
            for b in range(2):
                c = 2 * m.base + b
                r = residual(c, banks[2 * par + b], hn, lambda s: mod_g[:, l, 1, s, c:c + 1])
            r.then_inc(st.s_ev, 1)
            act.q.wait_ge(st.s_ev, G.plus(1))
            for b in range(2):
                add_square(2 * m.base + b, hn)

        pe.after(y_ready[-1])
        st.run(("out", l), multiply, evacuate)

        streams = 1 if last else 2
        ready = norm(streams, mod_coeff(l, 2))
        hid = hidden_s if last else hidden
        gate_up(("up2", l), streams * S, ready, u, hid)
        if l == 0:
            for n in range(3):
                mod_scales(1, n)
                mod_gates(1, n)
        down(("down2", l), streams * S, mod_gate(l, 2), hid)


    def final_norm(gain, dst):
        dve.after(norm_scale(S))
        clear_squares(S)
        return [dve.do(dve.q.scalar_tensor_tensor(out=dst(c), in0=h[:, c, 0:S], scalar=vcol(gain, c),
                                                  in1=banks[4][:, 0:S], op0=ALU.mult, op1=ALU.mult))
                for c in range(KC)]

    x2 = final_norm("norm_final", lambda c: h[:, c, 0:S])
    act.after(*x2)
    for c in range(KC):
        add_square(c, S)
    hidden_free = (st.s_pe, PHASE[("down2", L1 - 1)].first + 16)
    ready = norm(1, lambda c, s: (vcol("norm_mix_2", c), None))
    dve.after((st.s_ev, st.groups))
    act.after((st.s_ev, st.groups))

    ar = Arena()
    AR = ar.new("decayed_kk_r", [P, 4, NCH, 2, CH])
    o_at = 0
    tab = ar.new("tables_2", [P, CC.n - CC.kept])
    tables[0] = tab
    common_at = ar.at

    def load(dst, src, *marks):
        s = nc.alloc_semaphore("loaded_" + dst.name.split("_set")[0][:40])
        pool.after(*marks)
        pool.q.dma_start(dst, src).then_inc(s, 16)
        return (s, 16)

    tab2_ready = load(tab[:, :], ins["const"][:, CC.kept:CC.n], hidden_free)

    def simple_phase(name, multiply, evac):
        def evacuate(m, par, G, done):
            act.q.wait_ge(st.s_pe, at(done))
            dve.q.wait_ge(st.s_pe, at(done))
            evac(m.base, par).then_inc(st.s_ev, 1)
        st.run(name, multiply, evacuate, loop=False)
        marks = (st.s_ev, st.groups)
        for eng in (pe, act, dve):
            eng.after(marks)
        return marks

    first = [ready]

    def pair_multiply(par, part, slot):
        return pair_products(par, slot, u, S, first.pop() if first else None)

    mix = ar.new("mixed", [P, 14, S])
    dec = ar.new("decay", [P, 4, S])
    aa = ar.new("a", [P, 4, S])
    gg = ar.new("g", [P, 4, S])
    kk = ar.new("kk", [P, 4, S])
    bonus = ar.new("bonus", [P, 4, S])
    Pb = ar.new("decay_products", [P, 4, NCH, CH + 1])
    vT = ar.new("v_tokens", [P, 4, S])
    CP_at = ar.at
    CP = [ar.new(f"chunk_products{i}", [P, 4, NCH, 2, CH]) for i in range(2)]
    TT = ar.new("inverse_t", [P, 4, S])
    St, W1, U = [t[:, 0:4 * CH].rearrange("p (c t) -> p c t", c=4) for t in (sil[0], prod[0], prod[1])]
    assert ar.at <= arena_size - MAP_BYTES
    ar.at = CP_at
    wag = ar.new("w_a_g", [P, 1024])
    wag_ready = load(wag[:, :], ins["small"][:, SM_WA:SM_N], hidden_free)
    shift = [nc.alloc_sbuf_tensor_at(f"shifted{i}", [P, S + 1], F32, offset=ARENA_AT + CP_at + 8192 + 2048 * i)
             for i in range(2)]
    zs = [dve.do(dve.q.memset(shift[i][:, 0:1], 0.0)) for i in range(2)]
    dve.after(*zs)
    s_shift = nc.alloc_semaphore("projection_copied")
    s_mix = nc.alloc_semaphore("token_shift_mixed")
    s_dif = nc.alloc_semaphore("token_difference")
    def evac_rwkv(m, par):
        for b in range(2):
            c = 2 * m + b
            if c >= 2:
                act.q.wait_ge(s_mix, c - 1)
            x = act.q.activation(shift[b][:, 1:S + 1], banks[2 * par + b][:, 0:S], ACT.Copy)
            if b == 1:
                r = x
                dve.q.wait_ge(st.s_ev, groups0 + m + 1)
            else:
                x.then_inc(s_shift, 1)
                dve.q.wait_ge(s_shift, m + 1)
            dve.q.tensor_tensor(mix[:, c, :], shift[b][:, 0:S], shift[b][:, 1:S + 1], ALU.subtract).then_inc(s_dif, 1)
            dve.q.wait_ge(s_dif, c + 1)
            dve.q.scalar_tensor_tensor(out=mix[:, c, :], in0=mix[:, c, :], scalar=vcol("mu", c),
                                       in1=shift[b][:, 1:S + 1], op0=ALU.mult, op1=ALU.add).then_inc(s_mix, 1)
        return r

    groups0 = st.groups
    simple_phase("rwkv_in", pair_multiply, evac_rwkv)
    for eng in (pe, act, dve):
        eng.after((s_mix, 14))

    gate_ph = PHASE["gate_in"]
    s_gate = nc.alloc_semaphore("gates_evacuated")

    def gate_half(k, b):
        bank = banks[6 + k.base % 2]
        if b == 0:
            pe.q.wait_ge(st.s_lo, k.plus(gate_ph.first + 1))
            if not k.static() or k.base >= 2:
                pe.q.wait_ge(s_gate, k.plus(-1))
        slot = (gate_ph.first + k.base) % 2
        for kc in range(KC):
            r = three(bank[:, b * S:(b + 1) * S], tile_of(slot, b * KC + kc), chunk_of(u, kc, 0, S), kc == 0, kc == KC - 1)
        if b == 1:
            r.then_inc(st.s_pe, 1)

    def gate_side(k):
        if not k.static() or k.base + 1 < gate_ph.n:
            st.split(gate_ph, Count(k.base + 1, k.step, k.reg))
        else:
            st.split(PHASE["diff_in"], Count(0))
        act.q.wait_ge(st.s_pe, k.plus(gate_ph.first + 1))
        for b in range(2):
            c = k.times(2).plus(b)
            r = act.q.activation(gates[:, c, :], banks[6 + k.base % 2][:, b * S:(b + 1) * S], ACT.Sigmoid,
                                 bias=vec[:, bass.ds(c + VC.at["b_gate_2"], 1)])
        r.then_inc(s_gate, 1)

    def gate_panel(k):
        gate_half(Count(k), 0)
        gate_half(Count(k), 1)

    gate_panel(0)
    gate_side(Count(0))

    R, K_, V_ = mix[:, 0:4, :], mix[:, 4:8, :], mix[:, 8:12, :]
    F4 = 4 * S

    def flat4(t):
        return t.rearrange("p c t -> p (c t)")

    def V(ins, *marks):
        return dve.do(ins)

    def vec4(name, c):
        return vcol(name, c)

    m0 = act.do(act.q.activation(mix[0:64, 12, :], mix[0:64, 12, :], ACT.Tanh))
    m1 = act.do(act.q.activation(mix[:, 13, :], mix[:, 13, :], ACT.Sigmoid))
    pe.after(m0, m1, wag_ready)
    for c in range(4):
        z = pe.q.matmul(banks[c][:, 0:S], wag[0:64, c * P:(c + 1) * P], mix[0:64, 12, :], start=True, stop=True)
    zdone = pe.do(z)
    for c in range(4):
        z = pe.q.matmul(banks[4 + c // 2][:, (c % 2) * S:(c % 2 + 1) * S], wag[64:128, c * P:(c + 1) * P], mix[64:128, 12, :], start=True, stop=True)
    adone = pe.do(z)
    act.after(zdone)
    for c in range(4):
        sg = act.do(act.q.activation(dec[:, c, :], banks[c][:, 0:S], ACT.Sigmoid, bias=vcol("w0", c)))
    act.after(adone)
    for c in range(4):
        ag = act.do(act.q.activation(aa[:, c, :], banks[4 + c // 2][:, (c % 2) * S:(c % 2 + 1) * S],
                                       ACT.Sigmoid, bias=vcol("a0", c)))
    pe.after(sg)
    for c in range(4):
        z = pe.q.matmul(banks[c][:, 0:S], wag[:, 512 + c * P:512 + (c + 1) * P], mix[:, 13, :], start=True, stop=True)
    gdone = pe.do(z)
    act.after(gdone)
    for c in range(4):
        gg_done = act.do(act.q.activation(gg[:, c, :], banks[c][:, 0:S], ACT.Copy))
    act.after(sg)
    dc = act.do(act.q.activation(flat4(dec[:, :, :]), flat4(dec[:, :, :]), ACT.Exp, scale=-float(np.exp(-0.5))))

    for c in range(4):
        kk0 = dve.do(dve.q.tensor_scalar(kk[:, c, :], K_[:, c, :], vcol("k_k", c), None, ALU.mult))
    act.after(kk0)
    sqk = act.do(act.q.activation(flat4(vT[:, :, :]), flat4(kk[:, :, :]), ACT.Square))
    pe.after(sqk, ag)
    for c in range(4):
        z = pe.q.matmul(banks[4 + c // 2][:, (c % 2) * S:(c % 2 + 1) * S], cst("half_ones"), vT[:, c, :], start=True, stop=True)
    ssk = pe.do(z)
    gate_side(Count(1))
    gate_panel(1)
    act.after(ssk)
    for i in range(2):
        rtk = act.do(act.q.activation(flat4(vT[:, :, :])[:, 512 * i:512 * i + 512], banks[4 + i][:, :], ACT.Sqrt))
    dve.after(rtk)
    t = dve.do(dve.q.tensor_scalar(flat4(vT[:, :, :]), flat4(vT[:, :, :]), 1e-12, None, ALU.max))
    dve.after(t)
    t = dve.do(dve.q.reciprocal(flat4(vT[:, :, :]), flat4(vT[:, :, :])))
    dve.after(t)
    kkn = dve.do(dve.q.tensor_tensor(kk[:, :, :], kk[:, :, :], vT[:, :, :], ALU.mult))
    gate_side(Count(2))
    dve.after(ag, kkn)
    for c in range(4):
        t = dve.do(dve.q.tensor_scalar(vT[:, c, :], aa[:, c, :], -1.0, vcol("k_a", c), ALU.add, ALU.mult))
    dve.after(t)
    kp = dve.do(dve.q.scalar_tensor_tensor(out=flat4(K_), in0=flat4(vT[:, :, :]), scalar=1.0, in1=flat4(K_),
                                           op0=ALU.add, op1=ALU.mult))
    bb = dve.do(dve.q.tensor_tensor(aa[:, :, :], kk[:, :, :], aa[:, :, :], ALU.mult))
    dve.after(kp)
    for c in range(4):
        t = dve.do(dve.q.scalar_tensor_tensor(out=bonus[:, c, :], in0=R[:, c, :], scalar=vcol("r_k", c),
                                              in1=K_[:, c, :], op0=ALU.mult, op1=ALU.mult))
    gate_panel(2)
    pe.after(t, gg_done)
    for c in range(4):
        z = pe.q.matmul(banks[2 + c // 2][:, (c % 2) * S:(c % 2 + 1) * S], cst("half_ones"), bonus[:, c, :], start=True, stop=True)
    z = pe.do(z)
    dve.after(z)
    for i in range(2):
        bonus_done = dve.do(dve.q.tensor_tensor(flat4(bonus[:, :, :])[:, 512 * i:512 * i + 512], banks[2 + i][:, :],
                                                flat4(V_)[:, 512 * i:512 * i + 512], ALU.mult))
    z0 = dve.do(dve.q.memset(W1[:, 0, :], 0.0))
    z1 = dve.do(dve.q.memset(Pb[:, :, :, 0:1], 1.0))
    dve.after(z0, dc)
    for c in range(4):
        for k in range(NCH):
            t = dve.do(dve.q.tensor_tensor_scan(Pb[:, c, k, 1:CH + 1], dec[:, c, k * CH:(k + 1) * CH], W1[:, 0, :],
                                                1.0, ALU.mult, ALU.add))
    dve.after(t, z1, bb)

    def by_chunk(t):
        return t.rearrange("p c (k t) -> p c k t", k=NCH)

    pinv = []
    for c in range(4):
        pinv.append(dve.do(dve.q.reciprocal(by_chunk(dec[:, :, :])[:, c, :, :], Pb[:, c, :, 1:CH + 1])))
    for c in range(4):
        t1 = dve.do(dve.q.tensor_tensor(AR[:, c, :, 0, :], Pb[:, c, :, 0:CH], by_chunk(kk[:, :, :])[:, c], ALU.mult))
        t2 = dve.do(dve.q.tensor_tensor(AR[:, c, :, 1, :], Pb[:, c, :, 1:CH + 1], by_chunk(R)[:, c], ALU.mult))
    dve.after(*pinv)
    beta = dve.do(dve.q.tensor_tensor(aa[:, :, :], aa[:, :, :], dec[:, :, :], ALU.mult))
    kap = dve.do(dve.q.tensor_tensor(K_, K_, dec[:, :, :], ALU.mult))

    halves = [slice(0, 64), slice(64, 128)]

    def bank16(b0, c, k, hp, w=CH):
        x = (c * NCH + k) * w
        return banks[b0 + x // 512][halves[hp], x % 512:x % 512 + w]

    def both(fn):
        for c in range(4):
            for k in range(NCH):
                for hp in range(2):
                    r = fn(c, k, hp)
        return pe.do(r)

    def part(t, c, k, hp):
        return t[halves[hp], c, k * CH:(k + 1) * CH]

    gate_panel(3)
    gate_side(Count(3))
    pe.after((s_gate, 4))
    pe.after(beta, kap, t1, t2, bonus_done, gg_done, rtk)
    for i, src in enumerate((aa, mix)):
        off = 0 if i == 0 else 4
        z = both(lambda c, k, hp: pe.q.matmul(bank16(4 * i, c, k, hp, 2 * CH), part(src, c + off, k, hp),
                                              AR[halves[hp], c, k, :, :].rearrange("p a t -> p (a t)"),
                                              start=True, stop=True))
        dve.after(z)
        mask = cst("strict", 2 * CH).rearrange("p (o n) -> p o n", o=1).to_broadcast([P, NCH, 2 * CH])
        for c in range(4):
            mn_done = dve.do(dve.q.tensor_tensor(CP[i][:, c, :, :, :].rearrange("p k a t -> p k (a t)"),
                                                 banks[4 * i + c][:, :].rearrange("p (k n) -> p k n", k=NCH),
                                                 mask, ALU.mult))
    betaT, kapT = kk, R
    pe.after(mn_done, tab2_ready)
    id64 = [cst("ident")[halves[hp], 64 * hp:64 * hp + 64] for hp in range(2)]
    for i, (src, dst) in enumerate(((aa[:, :, :], betaT[:, :, :]), (K_, kapT), (V_, vT[:, :, :]))):
        z = both(lambda c, k, hp: pe.q.matmul(bank16(2 * i, c, k, hp), src[halves[hp], c, k * CH:(k + 1) * CH], id64[hp],
                                              start=True, stop=True))
        act.after(z, mn_done)
        for j in range(2):
            trd = act.do(act.q.activation(flat4(dst)[:, 512 * j:512 * j + 512], banks[2 * i + j][:, :], ACT.Copy))
    Tm, Xm, Mm = aa, dec, V_
    s_lm, s_lx, s_lc, s_lp, s_lt = [nc.alloc_semaphore(n) for n in
                                    ("level_masked", "level_mt", "level_mt_copied", "level_tmt", "level_added")]
    dve.after(trd)
    ident_rows = cst("ident64", CH).rearrange("p (o n) -> p o n", o=1).to_broadcast([P, 16, CH])

    def v16(t):
        return t.rearrange("p c (k t) -> p (c k) t", k=NCH)

    MabT = CP[0][:, :, :, 0, :].rearrange("p c k t -> p (c k) t")
    pe.after(trd)
    act.after(trd)

    def carry_wait():
        pe.q.matmul(banks[0][:, 0:1], cst("ident"), cst("ident", 1), start=True, stop=True)

    def masked(n):
        if not n.static() or n.base >= 1:
            dve.q.wait_ge(s_lx, n.plus(0))
        o = n.times(CH).plus(CC.at["level"] - CC.kept)
        lev = tab[:, bass.ds(o, CH)].rearrange("p (o n) -> p o n", o=1).to_broadcast([P, 16, CH])
        dve.q.tensor_tensor(v16(Mm), MabT, lev, ALU.mult).then_inc(s_lm, 1)

    def products(first_bank, left, right):
        for c in range(4):
            for k in range(NCH):
                for hp in range(2):
                    z = pe.q.matmul(bank16(first_bank, c, k, hp), part(left, c, k, hp), right(c, k, hp), start=True, stop=True)
        return z

    masked(Count(0))
    dve.q.wait_ge(s_lm, 1)
    e1 = dve.do(dve.q.tensor_tensor(v16(TT[:, :, :]), ident_rows, v16(Mm), ALU.subtract))
    pe.q.wait_ge(s_lm, 1)
    products(4, Mm, lambda c, k, hp: cst("ident64", CH)[halves[hp], :]).then_inc(s_lx, 1)
    dve.after(e1)
    masked(Count(1))
    for j in range(2):
        rows8 = cst("ident64", CH).rearrange("p (o n) -> p o n", o=1).to_broadcast([P, 8, CH])
        z = dve.q.tensor_tensor(v16(Tm[:, :, :])[:, 8 * j:8 * j + 8, :], rows8,
                                banks[4 + j][:, :].rearrange("p (x t) -> p x t", t=CH), ALU.subtract)
    z.then_inc(s_lt, 1)
    pe.after(e1)

    def level(n, k, final=False):
        dynamic = not n.static()
        pe.q.wait_ge(s_lm, n.plus(1))
        pe.q.wait_ge(s_lt, n.plus(0))
        if dynamic:
            carry_wait()
        products(0, Mm, lambda c, kk_, hp: part(Tm, c, kk_, hp)).then_inc(s_lx, 1)
        gate_half(k, 0)
        act.q.wait_ge(s_lx, n.plus(1))
        act.q.activation(flat4(Xm[:, :, :])[:, 0:512], banks[0][:, :], ACT.Copy)
        act.q.activation(flat4(Xm[:, :, :])[:, 512:1024], banks[1][:, :], ACT.Copy).then_inc(s_lc, 1)
        if not final:
            masked(Count(n.base + 1, n.step, n.reg))
        pe.q.wait_ge(s_lc, n.plus(0))
        if dynamic:
            carry_wait()
        if not final:
            products(2, TT, lambda c, kk_, hp: part(Xm, c, kk_, hp))
        products(4, Xm, lambda c, kk_, hp: part(TT, c, kk_, hp)).then_inc(s_lp, 1)
        gate_half(k, 1)
        gate_side(k)
        dve.q.wait_ge(s_lp, n.plus(0))
        for t_, first_bank in ((Tm, 2), (TT, 4))[final:]:
            for j in range(2):
                cols = slice(512 * j, 512 * j + 512)
                z = dve.q.tensor_tensor(flat4(t_[:, :, :])[:, cols], flat4(t_[:, :, :])[:, cols],
                                        banks[first_bank + j][:, :], ALU.subtract)
        z.then_inc(s_lt, 1)

    with nc.Fori(0, 2, engines=[mybir.EngineType.PE, mybir.EngineType.Activation, mybir.EngineType.DVE]) as n:
        for x in range(2):
            level(Count(1 + x, 2, n), Count(4 + x, 2, n))
    level(Count(5), Count(8), final=True)
    inverse_done = (s_lt, 6)
    YT = K_
    dve.after(inverse_done)
    s0 = dve.do(dve.q.memset(St[:, :, :], 0.0))
    pe.after(inverse_done, s0)
    act.after(inverse_done)

    def heads(fn):
        for c in range(4):
            for hp in range(2):
                r = fn(c, hp)
        return pe.do(r)

    def col4(b, c, hp):
        return banks[b][halves[hp], c * CH:(c + 1) * CH]

    state = s0
    ycopied = None
    for k in range(NCH):
        def w1(c, hp):
            pe.q.matmul(col4(0, c, hp), CP[1][halves[hp], c, k, 0, :], part(vT, c, k, hp), start=True, stop=False)
            return pe.q.matmul(col4(0, c, hp), AR[halves[hp], c, k, 0, :], St[halves[hp], c, :], start=False, stop=True)
        z = heads(w1)
        if k < 3:
            gate_half(Count(9 + k), 0)
        act.after(z)
        z = act.do(act.q.activation(W1[:, :, :].rearrange("p c t -> p (c t)"), banks[0][:, 0:256], ACT.Copy, scale=-1.0))
        pe.after(z)
        z = heads(lambda c, hp: pe.q.matmul(col4(1, c, hp), part(TT, c, k, hp), W1[halves[hp], c, :], start=True, stop=True))
        if k < 3:
            gate_half(Count(9 + k), 1)
        act.after(z)
        ud = act.do(act.q.activation(U[:, :, :].rearrange("p c t -> p (c t)"), banks[1][:, 0:256], ACT.Copy))
        pe.after(ud)

        def new_state(c, hp):
            pe.q.matmul(col4(3, c, hp), part(betaT, c, k, hp), U[halves[hp], c, :], start=True, stop=False)
            return pe.q.matmul(col4(3, c, hp), kapT[halves[hp], c, k * CH:(k + 1) * CH], part(vT, c, k, hp),
                               start=False, stop=True)
        ns = heads(new_state)
        pe.after(ycopied)

        def outputs(c, hp):
            pe.q.matmul(col4(2, c, hp), St[halves[hp], c, :], AR[halves[hp], c, k, 1, :], start=True, stop=False)
            pe.q.matmul(col4(2, c, hp), U[halves[hp], c, :], CP[0][halves[hp], c, k, 1, :], start=False, stop=False)
            return pe.q.matmul(col4(2, c, hp), part(vT, c, k, hp), CP[1][halves[hp], c, k, 1, :], start=False, stop=True)
        yd = heads(outputs)
        dve.after(ns, yd)
        t = dve.do(dve.q.tensor_tensor(St[:, :, :], banks[3][:, 0:256].rearrange("p (c t) -> p c t", c=4), St[:, :, :],
                                       ALU.add))
        dve.after(t)
        state = dve.do(dve.q.tensor_tensor(St[:, :, :], St[:, :, :],
                                           Pb[:, :, k, CH:CH + 1].to_broadcast([P, 4, CH]), ALU.mult))
        pe.after(state)
        act.after(yd)
        ycopied = act.do(act.q.activation(YT[:, :, k * CH:(k + 1) * CH],
                                          banks[2][:, 0:256].rearrange("p (c t) -> p c t", c=4), ACT.Copy))
        if k < 3:
            gate_side(Count(9 + k))
    pe.after(ycopied)
    for c in range(4):
        z = pe.q.matmul(banks[4 + c // 2][:, (c % 2) * S:(c % 2 + 1) * S], cst("half_ones"), YT[:, c, :], start=True, stop=True)
    z = pe.do(z)
    dve.after(z, ycopied)
    yf, sf = flat4(YT), flat4(vT[:, :, :])
    for i in range(2):
        cols = slice(512 * i, 512 * i + 512)
        cen = dve.do(dve.q.scalar_tensor_tensor(out=yf[:, cols], in0=banks[4 + i][:, :], scalar=-1.0 / HD,
                                                in1=yf[:, cols], op0=ALU.mult, op1=ALU.add))
    act.after(cen)
    z = act.do(act.q.activation(sf, yf, ACT.Square))
    pe.after(z, (s_gate, gate_ph.n))
    for c in range(4):
        z = pe.q.matmul(banks[6 + c // 2][:, (c % 2) * S:(c % 2 + 1) * S], cst("half_ones"), vT[:, c, :], start=True, stop=True)
    z = pe.do(z)
    act.after(z)
    for i in range(2):
        z = act.do(act.q.activation(sf[:, 512 * i:512 * i + 512], banks[6 + i][:, :], ACT.Sqrt, bias=cst("gn_eps", 1),
                                    scale=1.0 / HD))
    dve.after(z)
    z = dve.do(dve.q.reciprocal(sf, sf))
    dve.after(z)
    z = dve.do(dve.q.tensor_tensor(yf, yf, sf, ALU.mult))
    dve.after(z)
    for c in range(4):
        z = dve.do(dve.q.tensor_scalar(YT[:, c, :], YT[:, c, :], vcol("ln_w", c), vcol("ln_b", c), ALU.mult, ALU.add))
    dve.after(z)
    z = dve.do(dve.q.tensor_tensor(yf, yf, flat4(bonus[:, :, :]), ALU.add))
    dve.after(z)
    z = dve.do(dve.q.tensor_tensor(yf, yf, flat4(gg[:, :, :]), ALU.mult))
    dve.after(z)
    o_pl = Arena()
    o_hi = [o_pl.new("o_rwkv_hi", [P, 4, S], F32R)]
    o_lo = [o_pl.new("o_rwkv_lo", [P, 4, S], F32R)]

    def split_to(hi, lo, src, *marks):
        act.after(*marks)
        z = act.do(act.q.activation(hi, src, ACT.Copy))
        dve.after(z, *marks)
        return dve.do(dve.q.tensor_tensor(lo, src, hi.bitcast(F32), ALU.subtract))

    rw_done = split_to(o_hi[0][:, :, :], o_lo[0][:, :, :], YT, z)

    rwkv_over = [pe.last(), act.last(), dve.last()]
    ar.at = common_at
    o_hi.append(ar.new("o_mla_hi", [P, 4, S], F32R))
    o_lo.append(ar.new("o_mla_lo", [P, 4, S], F32R))
    o_hi.append(ar.new("o_diff_hi", [P, 4, S], F32R))
    o_lo.append(ar.new("o_diff_lo", [P, 4, S], F32R))
    scratch_at = ar.at
    qd = ar.new("diff_q", [P, DH, S])
    kd = ar.new("diff_k", [P, DH, S])
    vd = ar.new("diff_v", [P, 2, 512])
    lamt = ar.new("lambda_products", [P, 2 * HD])
    lam = ar.new("lambda", [P, 4])
    probs = [ar.new(f"diff_probs{i}", [P, 2, S]) for i in range(N_PROBS)]
    probs_t = [ar.new(f"diff_probs_t{i}", [P, 2, S]) for i in range(2)]
    for eng in (pe, act, dve):
        eng.after(*rwkv_over)

    dve.after(map_ready, tab2_ready, loaded)
    for o in (0, 2 * P):
        t = dve.do(dve.q.tensor_tensor(rel[:, :, o:o + P], rel[:, :, o:o + P],
                                       cst("causal").rearrange("p (o k) -> p o k", o=1).to_broadcast([P, DH, P]), ALU.add))
    rel_ready = t
    lv = vcol("lambda", 0, 4 * HD).rearrange("p (a b d) -> p a b d", a=2, b=2)
    t = dve.do(dve.q.tensor_tensor(lamt[:, :].rearrange("p (a d) -> p a d", a=2), lv[:, :, 0, :], lv[:, :, 1, :], ALU.mult))
    dve.after(t)
    t = dve.do(dve.q.tensor_reduce(out=lam[:, 0:2], in_=lamt[:, :].rearrange("p (a d) -> p a d", a=2), axis=AX.X, op=ALU.add))
    act.after(t)
    t = act.do(act.q.activation(lam[:, 0:2], lam[:, 0:2], ACT.Exp))
    dve.after(t)
    t = dve.do(dve.q.tensor_tensor(lam[:, 2:3], lam[:, 1:2], lam[:, 0:1], ALU.subtract))
    dve.after(t)
    lam_ready = dve.do(dve.q.tensor_scalar(lam[:, 3:4], lam[:, 2:3], -LAMBDA_INIT, None, ALU.add))

    def wide_multiply(par, part, slot):
        for t in range(2):
            for kc in range(KC):
                w = (whi[slot][:, kc * 256:(kc + 1) * 256], wlo[slot][:, kc * 256:(kc + 1) * 256])
                r = three(banks[2 * par][:, 256 * t:256 * t + 256], chunk_of(u, kc, t * P, t * P + P), w,
                          kc == 0, kc == KC - 1)
        return r

    order = [0]

    def diff_multiply(par, part, slot):
        order[0] += 1
        return (pair_multiply if order[0] <= 4 else wide_multiply)(par, part, slot)

    def evac_diff(m, par):
        if m >= 4:
            return act.q.activation(vd[:, :, (m - 4) * 256:(m - 3) * 256],
                                    banks[2 * par][:, :].rearrange("p (t c) -> p t c", t=2), ACT.Copy)
        dst, c = (qd, 2 * m) if m < 2 else (kd, 2 * m - 4)
        for b in range(2):
            r = act.q.activation(dst[:, c + b, :], banks[2 * par + b][:, 0:S], ACT.Copy,
                                 scale=HD ** -0.5 if m < 2 else 1.0)
        return r

    diff_in = simple_phase("diff_in", diff_multiply, evac_diff)

    def causal_attention(name, units, score, prepare, n_maps, pv, stat):
        mk = [dict() for _ in units]
        free = {}

        def scores(i):
            uu = units[i]
            if i >= 2:
                pe.after(mk[i - 2]["exp"])
            for m in range(n_maps):
                r = score(uu, m, banks[4 + 2 * (i % 2) + m])
            mk[i]["scores"] = pe.do(r)

        def exponentials(i):
            uu = units[i]
            qt = uu[-1]
            nk = (qt + 1) * P
            k = i % 2
            st_ = stat[:, k, :]
            dve.after(mk[i]["scores"], mk[i - 2]["norm"] if i >= 2 else None)
            act.after(mk[i - N_PROBS]["transposed"] if i >= N_PROBS else None)
            for m in range(n_maps):
                bank = banks[4 + 2 * k + m]
                dve.after(prepare(uu, m, bank))
                t = dve.do(dve.q.tensor_reduce(out=st_[:, m:m + 1], in_=bank[:, 0:nk], axis=AX.X, op=ALU.max, negate=True))
                if name == "mla":
                    dve.after(t)
                    t = dve.do(dve.q.tensor_scalar(st_[:, m:m + 1], st_[:, m:m + 1], MLA_SCALE, None, ALU.mult))
                act.after(t)
                ex = act.do(act.q.activation(probs[i % N_PROBS][:, m, 0:nk], bank[:, 0:nk], ACT.Exp, bias=st_[:, m:m + 1],
                                             scale=MLA_SCALE if name == "mla" else 1.0, accum_out=st_[:, 2 + m:3 + m]))
            mk[i]["exp"] = ex

        def normalise(i):
            nk = (units[i][-1] + 1) * P
            k = i % 2
            st_ = stat[:, k, :]
            dve.after(mk[i]["exp"])
            t = dve.do(dve.q.reciprocal(st_[:, 4:4 + n_maps], st_[:, 2:2 + n_maps]))
            dve.after(t)
            if n_maps == 2:
                t = dve.do(dve.q.tensor_tensor(st_[:, 5:6], st_[:, 5:6], lam[:, 3:4], ALU.mult))
                dve.after(t)
            t = dve.do(dve.q.tensor_scalar(probs[i % N_PROBS][:, 0, 0:nk], probs[i % N_PROBS][:, 0, 0:nk], st_[:, 4:5], None, ALU.mult))
            if n_maps == 2:
                dve.after(t)
                t = dve.do(dve.q.scalar_tensor_tensor(out=probs[i % N_PROBS][:, 0, 0:nk], in0=probs[i % N_PROBS][:, 1, 0:nk],
                                                      scalar=st_[:, 5:6], in1=probs[i % N_PROBS][:, 0, 0:nk],
                                                      op0=ALU.mult, op1=ALU.add))
            mk[i]["norm"] = t

        def transposes(i):
            qt = units[i][-1]
            pe.after(mk[i]["norm"], mk[i - 2]["copied"] if i >= 2 else None)
            for t in range(qt + 1):
                r = pe.q.transpose(banks[i % 2][:, t * P:(t + 1) * P], probs[i % N_PROBS][:, 0, t * P:(t + 1) * P], cst("ident"))
            mk[i]["transposed"] = pe.do(r)
            act.after(mk[i]["transposed"], mk[i - 3 - i % 2 + 1 - 1].get("pv") if i >= 4 else None,
                      mk[(i // 2) * 2 - 3].get("pv") if i >= 4 else None)
            mk[i]["copied"] = act.do(act.q.activation(
                probs_t[(i // 2) % 2][:, 0:qt + 1, qt * P:(qt + 1) * P],
                banks[i % 2][:, 0:(qt + 1) * P].rearrange("p (t q) -> p t q", t=qt + 1), ACT.Copy))

        def values(i):
            if units[i][-1] == 0:
                return
            pair = i // 2
            pe.after(mk[i]["copied"], mk[i - 1]["copied"], free.get(pair - 2))
            r = pv(units[i], probs_t[pair % 2], banks[2 + pair % 2])
            mk[i]["pv"] = pe.do(r)
            free[pair] = finish_head(name, units[i], banks[2 + pair % 2], mk[i]["pv"])

        scores(0)
        for i in range(len(units) + 3):
            if i + 1 < len(units):
                scores(i + 1)
            if i < len(units):
                exponentials(i)
            if 1 <= i <= len(units):
                normalise(i - 1)
            if 2 <= i < len(units) + 2:
                transposes(i - 2)
            if i >= 3:
                values(i - 3)
        return list(free.values())

    diff_out = ar.new("diff_out", [P, DH, S])
    diff_stat = ar.new("diff_stat", [P, 2, 8])

    def finish_head(name, uu, bank, mark):
        if name == "diff":
            act.after(mark)
            return act.do(act.q.activation(diff_out[:, uu[0], :], bank[:, 0:S], ACT.Copy))
        hh = uu[0]
        rows_ = halves[hh % 2]
        dve.after(mark)
        t = dve.do(dve.q.tensor_copy(o_hi[1][rows_, hh // 2, :], bank[rows_, 0:S]))
        dve.after(t)
        return dve.do(dve.q.tensor_tensor(o_lo[1][rows_, hh // 2, :], bank[rows_, 0:S],
                                          o_hi[1][rows_, hh // 2, :].bitcast(F32), ALU.subtract))

    def diff_score(uu, m, bank):
        hh, qt = uu
        return pe.q.matmul(bank[:, 0:(qt + 1) * P], qd[halves[m], hh, qt * P:(qt + 1) * P],
                           kd[halves[m], hh, 0:(qt + 1) * P], start=True, stop=True)

    def diff_prepare(uu, m, bank):
        hh, qt = uu
        w = (qt + 1) * P
        return dve.do(dve.q.tensor_tensor(bank[:, 0:w], bank[:, 0:w], rel[:, hh, qt * P:qt * P + w], ALU.add))

    def diff_pv(uu, pt, bank):
        hh, _ = uu
        pe.q.matmul(bank[:, 0:S], vd[:, 0, hh * P:(hh + 1) * P], pt[:, 0, :], start=True, stop=False)
        return pe.q.matmul(bank[:, P:S], vd[:, 1, hh * P:(hh + 1) * P], pt[:, 1, P:S], start=False, stop=True)

    dve.after(rel_ready, lam_ready)
    heads_done = causal_attention("diff", [(hh, qt) for hh in range(DH) for qt in range(2)], diff_score,
                                  diff_prepare, 2, diff_pv, diff_stat)
    act.after(*heads_done)
    dve.after(*heads_done)
    t = act.do(act.q.activation(qd[:, :, :], diff_out[:, :, :], ACT.Square))
    gain = dve.do(dve.q.tensor_scalar(lam[:, 0:1], vcol("subln"), 1.0 - LAMBDA_INIT, None, ALU.mult))
    pe.after(t)
    for i in range(2):
        z = pe.q.matmul(banks[i][:, :], cst("ones"), qd[:, 2 * i:2 * i + 2, :], start=True, stop=True)
    z = pe.do(z)
    act.after(z)
    for i in range(2):
        z = act.do(act.q.activation(flat4(qd[:, :, :])[:, 512 * i:512 * i + 512], banks[i][:, :], ACT.Sqrt,
                                    bias=cst("sub_eps", 1), scale=1.0 / P))
    dve.after(z, gain)
    z = dve.do(dve.q.reciprocal(flat4(qd[:, :, :]), flat4(qd[:, :, :])))
    dve.after(z)
    z = dve.do(dve.q.scalar_tensor_tensor(out=flat4(diff_out[:, :, :]), in0=flat4(diff_out[:, :, :]), scalar=lam[:, 0:1],
                                          in1=flat4(qd[:, :, :]), op0=ALU.mult, op1=ALU.mult))
    diff_done = split_to(o_hi[2][:, :, :], o_lo[2][:, :, :], diff_out[:, :, :], z)

    ar.at = scratch_at
    smalls = ar.new("uq_ukv", [P, SM_WA])
    prow = ar.new("pos_row_m", [P, S], I32)
    cq = ar.new("c_q", [P, 2, S])
    ckv = ar.new("c_kv", [P, S])
    krr = ar.new("k_rope", [P, 2, S])
    Q = ar.new("mla_q", [P, MH, S])
    K2 = ar.new("mla_k", [P, MH, S])
    vm = ar.new("mla_v", [P, 2, 512])
    trig = ar.new("trig", [P, 4, S])
    probs = [ar.new(f"mla_probs{i}", [P, 1, S]) for i in range(N_PROBS)]
    probs_t = [ar.new(f"mla_probs_t{i}", [P, 2, S]) for i in range(2)]
    mla_stat = ar.new("mla_stat", [P, 2, 8])
    diff_over = [pe.last(), act.last(), dve.last()]
    for eng in (pe, act, dve):
        eng.after(*diff_over)
    sm_ready = load(smalls[:, :], ins["small"][:, 0:SM_WA], diff_over)
    pr_ready = load(prow[:, :], ins["pos_row"], diff_over)

    rp = slice(64, 96)
    ang, turns, cos_t, sin_t = [trig[rp, i, :] for i in range(4)]
    dve.after(pr_ready)
    z = dve.do(dve.q.tensor_copy(ang, prow[rp, :]))
    dve.after(z)
    z = dve.do(dve.q.tensor_scalar(ang, ang, cst("inv_freq", 1)[rp], None, ALU.mult))
    dve.after(z)
    z = dve.do(dve.q.tensor_scalar(turns, ang, float(np.float32(1 / (2 * np.pi))), ROUND, ALU.mult, ALU.add))
    dve.after(z)
    z = dve.do(dve.q.tensor_scalar(turns, turns, ROUND, None, ALU.subtract))
    for part_of_turn in TWO_PI:
        dve.after(z)
        z = dve.do(dve.q.scalar_tensor_tensor(out=ang, in0=turns, scalar=-part_of_turn, in1=ang, op0=ALU.mult, op1=ALU.add))
    dve.after(z)
    pi = float(np.nextafter(np.float32(np.pi), np.float32(0)))
    z = dve.do(dve.q.tensor_scalar(ang, ang, pi, -pi, ALU.min, ALU.max))
    act.after(z)
    z = act.do(act.q.activation(cos_t, ang, ACT.Abs))
    dve.after(z)
    z = dve.do(dve.q.tensor_scalar(cos_t, cos_t, -1.0, float(np.pi / 2), ALU.mult, ALU.add))
    act.after(z)
    z1 = act.do(act.q.activation(cos_t, cos_t, ACT.Sin))
    z2 = act.do(act.q.activation(sin_t, ang, ACT.Sin))
    dve.after(z1, z2)
    trig_ready = dve.do(dve.q.tensor_scalar(sin_t, sin_t, cst("rope_sign", 1)[rp], None, ALU.mult))
    dve.after(trig_ready)

    order[0] = 0

    def mla_multiply(par, part, slot):
        order[0] += 1
        if order[0] == 1:
            return pair_multiply(par, part, slot)
        for kc in range(KC):
            three(banks[2 * par][:, 0:S], tile_of(slot, kc), chunk_of(u, kc, 0, S), kc == 0, kc == KC - 1)
        for x in range(2):
            for kc in range(KC):
                o = (KC + kc) * P + 32 * x
                r = three(banks[2 * par + 1][0:96, x * S:x * S + S], (whi[slot][:, o:o + 96], wlo[slot][:, o:o + 96]),
                          chunk_of(u, kc, 0, S), kc == 0, kc == KC - 1)
        return r

    def evac_mla(m, par):
        if m == 0:
            for b in range(2):
                r = act.q.activation(cq[:, b, :], banks[2 * par + b][:, 0:S], ACT.Copy)
            return r
        act.q.activation(ckv[:, :], banks[2 * par][:, 0:S], ACT.Copy)
        return act.q.activation(krr[rp, :, :], banks[2 * par + 1][rp, :].rearrange("p (x t) -> p x t", x=2), ACT.Copy)

    simple_phase("mla_in", mla_multiply, evac_mla)
    z = dve.do(dve.q.tensor_tensor(krr[rp, 0, :], krr[rp, 0, :], cos_t, ALU.mult))
    z2 = dve.do(dve.q.tensor_tensor(krr[rp, 1, :], krr[rp, 1, :], sin_t, ALU.mult))
    dve.after(z, z2)
    kr_done = dve.do(dve.q.tensor_tensor(
        K2[rp, :, :], krr[rp, 0:1, :].to_broadcast([32, MH, S]), krr[rp, 1:2, :].to_broadcast([32, MH, S]), ALU.add))
    sq1 = act.do(act.q.activation(Q[:, 0:2, :], cq[:, :, :], ACT.Square))
    sq2 = act.do(act.q.activation(Q[:, 2, :], ckv[:, :], ACT.Square))
    pe.after(sq1, sq2)
    for i in range(2):
        z = pe.q.matmul(banks[4][:, 0:S], cst("ones"), Q[:, i, :], start=(i == 0), stop=(i == 1))
    z = pe.do(pe.q.matmul(banks[5][:, 0:S], cst("ones"), Q[:, 2, :], start=True, stop=True))
    act.after(z)
    z1 = act.do(act.q.activation(Q[:, 3, :], banks[4][:, 0:S], ACT.Sqrt, bias=cst("eps", 1), scale=1.0 / (2 * P)))
    z2 = act.do(act.q.activation(Q[:, 4, :], banks[5][:, 0:S], ACT.Sqrt, bias=cst("eps", 1), scale=1.0 / P))
    dve.after(z1, z2)
    z = dve.do(dve.q.reciprocal(Q[:, 3:5, :], Q[:, 3:5, :]))
    dve.after(z)
    for i in range(2):
        z = dve.do(dve.q.scalar_tensor_tensor(out=cq[:, i, :], in0=cq[:, i, :], scalar=vcol("mla_q_norm", i),
                                              in1=Q[:, 3, :], op0=ALU.mult, op1=ALU.mult))
    lat = dve.do(dve.q.scalar_tensor_tensor(out=ckv[:, :], in0=ckv[:, :], scalar=vcol("mla_kv_norm"),
                                            in1=Q[:, 4, :], op0=ALU.mult, op1=ALU.mult))
    pe.after(lat, z, sm_ready)
    act.after(lat)
    uq = smalls[:, SM_UQ:SM_UKV].rearrange("p (k h c) -> p k h c", k=2, h=MH)
    ukv = smalls[:, SM_UKV:SM_WA].rearrange("p (x n) -> p x n", x=2)
    qfree = [None, None]
    for hh in range(MH):
        b = 2 * (hh % 2)
        pe.after(qfree[hh % 2])
        for i in range(2):
            pe.q.matmul(banks[b][0:96, 0:S], uq[:, i, hh, 0:96], cq[:, i, :], start=(i == 0), stop=(i == 1))
        for i in range(2):
            pe.q.matmul(banks[b + 1][rp, 0:S], uq[:, i, hh, 96:128], cq[:, i, :], start=(i == 0), stop=(i == 1))
        zq = pe.do(pe.q.matmul(banks[b + 4][0:64, 0:S], ukv[:, 0, hh * MN:(hh + 1) * MN], ckv[:, :], start=True, stop=True))
        act.after(zq)
        a1 = act.do(act.q.activation(Q[0:64, hh, :], banks[b][0:64, 0:S], ACT.Copy))
        a2 = act.do(act.q.activation(K2[0:64, hh, :], banks[b + 4][0:64, 0:S], ACT.Copy))
        dve.after(zq)
        d1 = dve.do(dve.q.tensor_tensor(Q[rp, hh, :], banks[b][rp, 0:S], cos_t, ALU.mult))
        d2 = dve.do(dve.q.tensor_tensor(krr[rp, hh % 2, :], banks[b + 1][rp, 0:S], sin_t, ALU.mult))
        dve.after(d1, d2)
        d3 = dve.do(dve.q.tensor_tensor(Q[rp, hh, :], Q[rp, hh, :], krr[rp, hh % 2, :], ALU.add))
        qfree[hh % 2] = [a2, d3]
    for t in range(2):
        pe.after(qfree)
        z = pe.q.matmul(banks[6 + t][:, :], ckv[:, t * P:(t + 1) * P], ukv[:, 1, :], start=True, stop=True)
    z = pe.do(z)
    act.after(z)
    for t in range(2):
        vm_done = act.do(act.q.activation(vm[:, t, :], banks[6 + t][:, :], ACT.Copy))
    pe.after(vm_done, kr_done)

    def mla_score(uu, m, bank):
        hh, qt = uu
        return pe.q.matmul(bank[:, 0:(qt + 1) * P], Q[0:96, hh, qt * P:(qt + 1) * P], K2[0:96, hh, 0:(qt + 1) * P],
                           start=True, stop=True)

    def mla_prepare(uu, m, bank):
        hh, qt = uu
        return dve.do(dve.q.tensor_tensor(bank[:, qt * P:(qt + 1) * P], bank[:, qt * P:(qt + 1) * P], cst("causal"), ALU.add))

    def mla_pv(uu, pt, bank):
        hh, _ = uu
        rows_ = halves[hh % 2]
        pe.q.matmul(bank[rows_, 0:S], vm[:, 0, hh * HD:(hh + 1) * HD], pt[:, 0, :], start=True, stop=False)
        return pe.q.matmul(bank[rows_, P:S], vm[:, 1, hh * HD:(hh + 1) * HD], pt[:, 1, P:S], start=False, stop=True)

    mla_done = causal_attention("mla", [(hh, qt) for hh in range(MH) for qt in range(2)], mla_score, mla_prepare,
                                1, mla_pv, mla_stat)

    ar.at = scratch_at
    mla_over = [pe.last(), act.last(), dve.last()] + mla_done
    for eng in (pe, act, dve):
        eng.after(*mla_over)

    s_br = nc.alloc_semaphore("branch_merged")

    def branch_multiply(par, part, slot):
        for b in range(3):
            for kc in range(4):
                r = three(banks[2 * par + b // 2][:, (b % 2) * S:(b % 2 + 1) * S], tile_of(slot, b * 4 + kc),
                          chunk_of((o_hi[b], o_lo[b]), kc, 0, S), kc == 0, kc == 3)
        return r

    def branch_evac(m, par, G, done):
        dve.q.wait_ge(st.s_pe, at(done))
        c = at(m)
        k = Count(4 * m.base, 4 * m.step, m.reg)
        if not m.static() or m.base >= 2:
            dve.q.wait_ge(s_hh, hidden_count[0] + m.plus(-1))
        dve.q.tensor_tensor(prod[par][:, 0:S], banks[2 * par][:, 0:S], gates[:, c, :], ALU.mult).then_inc(s_br, 1)
        dve.q.tensor_tensor(sil[par][:, 0:S], banks[2 * par][:, S:2 * S], gates[:, c + KC, :], ALU.mult).then_inc(s_br, 1)
        dve.q.tensor_tensor(sil[par][:, S:2 * S], banks[2 * par + 1][:, 0:S], gates[:, c + 2 * KC, :], ALU.mult).then_inc(s_br, 1)
        dve.q.wait_ge(s_br, k.plus(2))
        dve.q.wait_ge(s_br, k.plus(3))
        dve.q.tensor_tensor(prod[par][:, 0:S], prod[par][:, 0:S], sil[par][:, 0:S], ALU.add).then_inc(s_br, 1)
        dve.q.wait_ge(s_br, k.plus(4))
        dve.q.tensor_tensor(prod[par][:, 0:S], prod[par][:, 0:S], sil[par][:, S:2 * S], ALU.add).then_inc(st.s_ev, 1)

    h0 = hidden_count[0]
    st.run("branch", branch_multiply, branch_evac, finish_hidden(S, (u_hi, u_lo), h0))
    hidden_count[0] += KC
    pe.after((s_hl, hidden_count[0]))

    def wo_evac(m, par, G, done):
        dve.q.wait_ge(st.s_pe, at(done))
        for b in range(2):
            r = residual(2 * m.base + b, banks[2 * par + b], S, lambda s: 1.0)
        r.then_inc(st.s_ev, 1)
        act.q.wait_ge(st.s_ev, G.plus(1))
        for b in range(2):
            add_square(2 * m.base + b, S)

    root_table()
    st.run("w_o", pair_multiply, wo_evac)
    ready = norm(1, lambda c, s: (vcol("norm_ffn_2", c), None))

    over = [pe.last(), act.last(), (st.s_pe, st.panels_done("w_o"))]
    cu = [nc.alloc_sbuf_tensor_at(f"conv_in{i}", [P, 2, S + 2], F32, offset=ARENA_AT + 49152 + 8192 * i) for i in range(2)]
    cv = [nc.alloc_sbuf_tensor_at(f"conv_out{i}", [P, 2, S], F32, offset=ARENA_AT + 49152 + 4096 + 8192 * i) for i in range(2)]
    hid2 = [nc.alloc_sbuf_tensor_at(f"hid2_{i}", [P, FC, S], F32R, offset=ARENA_AT + 22528 * i) for i in range(2)]
    act.after(*over)
    dve.after(*over)
    zs = [dve.do(dve.q.memset(cu[i][:, :, 0:2], 0.0)) for i in range(2)]
    dve.after(*zs)
    s_cu, s_cv, s_tap, s_cs, s_cp = [nc.alloc_semaphore(n) for n in (
        "conv_in_copied", "conv_last_tap", "conv_tap", "conv_gate_activated", "conv_product")]
    h0 = hidden_count[0]
    first.append(ready)

    def vdyn(name, m, b):
        o = VC.at[name] + b * FC + m.base
        return vec[:, o:o + 1] if m.static() else vec[:, bass.ds(m.reg * m.step + o, 1)]

    def up_evac(m, par, G, done):
        act.q.wait_ge(st.s_pe, at(done))
        if not m.static() or m.base >= 2:
            act.q.wait_ge(s_tap, m.times(4).plus(-4))
            act.q.wait_ge(s_cp, m.plus(-1))
        for b in range(2):
            act.q.activation(cu[par][:, b, 2:S + 2], banks[2 * par + b][:, 0:S], ACT.Copy)
        for b in range(2):
            r = act.q.activation(cv[par][:, b, :], banks[2 * par + b][:, 0:S], ACT.Identity,
                                 scale=vdyn(("conv_w", 2), m, b), bias=vdyn("conv_b", m, b))
        r.then_inc(st.s_ev, 1)
        dve.q.wait_ge(st.s_ev, G.plus(1))
        for tap in (1, 0):
            for b in range(2):
                if tap == 0:
                    dve.q.wait_ge(s_tap, m.times(4).plus(1 + b))
                dve.q.scalar_tensor_tensor(out=cv[par][:, b, :], in0=cu[par][:, b, tap:tap + S],
                                           scalar=vdyn(("conv_w", tap), m, b), in1=cv[par][:, b, :],
                                           op0=ALU.mult, op1=ALU.add).then_inc(s_tap, 1)

    def up_product(m, par):
        act.q.wait_ge(s_tap, m.times(4).plus(3))
        act.q.activation(sil[par][:, 0:S], cv[par][:, 0, :], ACT.Silu).then_inc(s_cs, 1)
        dve.q.wait_ge(s_cs, m.plus(1))
        dve.q.wait_ge(s_tap, m.times(4).plus(4))
        if not m.static() or m.base >= 2:
            dve.q.wait_ge(s_hh, Count(h0 + m.base, m.step, m.reg).plus(-1))
        dve.q.tensor_tensor(prod[par][:, 0:S], sil[par][:, 0:S], cv[par][:, 1, :], ALU.mult).then_inc(s_cp, 1)

    def up_hidden(m, par):
        k = Count(h0 + m.base, m.step, m.reg)
        act.q.wait_ge(s_cp, m.plus(1))
        act.q.activation(hid2[0][:, at(m), :], prod[par][:, 0:S], ACT.Copy).then_inc(s_hh, 1)
        dve.q.wait_ge(s_hh, k.plus(1))
        dve.q.tensor_tensor(hid2[1][:, at(m), :], prod[par][:, 0:S], hid2[0][:, at(m), :].bitcast(F32),
                            ALU.subtract).then_inc(s_hl, 1)

    st.run("up_2", pair_multiply, up_evac, second=up_product, third=up_hidden)
    hidden_count[0] += FC
    pe.after((s_hl, hidden_count[0]))
    q0 = sq_count[0]

    def down2_multiply(par, part, slot):
        for t in range(11):
            kc = part * 11 + t
            r = three(banks[2 * par][:, 0:S], tile_of(slot, t), chunk_of(hid2, kc, 0, S), kc == 0, kc == FC - 1)
        return r

    def down2_evac(m, par, G, done):
        dve.q.wait_ge(st.s_pe, at(done))
        residual(at(m), banks[2 * par], S, lambda s: 1.0).then_inc(st.s_ev, 1)
        act.q.wait_ge(st.s_ev, G.plus(1))
        add_square(at(m), S, count=Count(q0 + m.base, m.step, m.reg))

    root_table()
    st.run("down_2", down2_multiply, down2_evac, ppg=2)
    sq_count[0] += KC
    y = final_norm("norm_final_2", lambda c: h[:, c, 0:S])
    nc.sync.wait_ge(*y[-1])
    s_out = nc.alloc_semaphore("result_stored")
    nc.sync.dma_start(out, h[:, :, 0:S]).then_inc(s_out, 16)
    nc.sync.wait_ge(s_out, 16)


def kernel(**inputs):
    import concourse.bacc as _bacc
    from concourse.bass_utils import run_bass_kernel_spmd as _run

    arrays = {"in_" + k: a for k, a in lay_out(inputs).items()}
    nc = _bacc.Bacc("TRN2", target_bir_lowering=False, num_devices=1)
    ins = {k[3:]: nc.dram_tensor(k, a.shape, mybir.dt.from_np(a.dtype), kind="ExternalInput").ap()
           for k, a in arrays.items()}
    out = nc.dram_tensor("out", [P, KC, S], F32, kind="ExternalOutput").ap()
    build(nc, ins, out)
    r = _run(nc, [arrays], core_ids=[0])
    got = r.results[0]["out"]
    return got.transpose(2, 1, 0).reshape(1, S, D)
```
